# Optimizing a Trainium2 kernel written in Bass

```python
import math
import jax, jax.numpy as jnp
from jax import lax
import numpy as np

D_MODEL = 2048
BATCH = 1
SEQ = 256
DEPTH = 2

CHUNK = 64
N_MIXERS = 2
N_LAYERS_A = (DEPTH + 1) // 2
N_LAYERS_B = DEPTH // 2

HEAD_DIM = 64
N_Q_HEADS = D_MODEL // HEAD_DIM
N_KV_HEADS = max(4, N_Q_HEADS // 8)
GQA_GROUP = N_Q_HEADS // N_KV_HEADS
WINDOW = 128
WIN_CHUNKS = WINDOW // CHUNK
QKV_WIDTH = (N_Q_HEADS + 2 * N_KV_HEADS) * HEAD_DIM

SGU_CHUNK = 128
SGU_WIDTH = D_MODEL
SGU_GROUPS = 16
SGU_GROUP_DIM = SGU_WIDTH // SGU_GROUPS

D_FF = -(-8 * D_MODEL // (3 * 256)) * 256

N_MOD = 6
EPS = 1e-6
NEG_INF = -1e30

kernel_name = "hybrid_swa_sink_gmlp_adaln_trunk"

def _rms(x):
    xf = x.astype(jnp.float32)
    y = xf * lax.rsqrt(jnp.mean(xf * xf, axis=-1, keepdims=True) + EPS)
    return y.astype(x.dtype)

def _modulate(x, shift, scale):
    return _rms(x) * (1 + scale[:, None, :]) + shift[:, None, :]

def _alibi_slopes(n):
    return jnp.asarray(2.0 ** (-8.0 * np.arange(1, n + 1) / n), dtype=jnp.float32)

def sliding_window_attention(h, w_qkv, q_gain, k_gain, sinks, w_o):
    B, S, _ = h.shape
    nC = S // CHUNK
    qkv = h @ w_qkv
    q, k, v = jnp.split(qkv, [N_Q_HEADS * HEAD_DIM, (N_Q_HEADS + N_KV_HEADS) * HEAD_DIM], axis=-1)
    q = q.reshape(B, nC, CHUNK, N_KV_HEADS, GQA_GROUP, HEAD_DIM)
    k = k.reshape(B, nC, CHUNK, N_KV_HEADS, HEAD_DIM)
    v = v.reshape(B, nC, CHUNK, N_KV_HEADS, HEAD_DIM)
    q = _rms(q) * q_gain
    k = _rms(k) * k_gain
    pad = jnp.zeros_like(k[:, : WIN_CHUNKS - 1])
    kp = jnp.concatenate([pad, k], axis=1)
    vp = jnp.concatenate([jnp.zeros_like(v[:, : WIN_CHUNKS - 1]), v], axis=1)
    kb = jnp.concatenate([kp[:, j:j + nC] for j in range(WIN_CHUNKS)], axis=2)
    vb = jnp.concatenate([vp[:, j:j + nC] for j in range(WIN_CHUNKS)], axis=2)

    s = jnp.einsum('bnqhgd,bnkhd->bnhgqk', q.astype(jnp.float32), kb.astype(jnp.float32))
    s = s * (HEAD_DIM ** -0.5)
    qi = np.arange(CHUNK)[:, None]
    kl = np.arange(WIN_CHUNKS * CHUNK)[None, :]
    dist = jnp.asarray(np.abs(qi + (WIN_CHUNKS - 1) * CHUNK - kl), dtype=jnp.float32)
    slopes = _alibi_slopes(N_Q_HEADS).reshape(N_KV_HEADS, GQA_GROUP)
    s = s - slopes[:, :, None, None] * dist
    key_chunk = np.arange(nC)[:, None] - (WIN_CHUNKS - 1) + np.arange(WIN_CHUNKS * CHUNK)[None, :] // CHUNK
    valid = jnp.asarray(key_chunk >= 0)
    s = jnp.where(valid[None, :, None, None, None, :], s, NEG_INF)
    sink = jnp.broadcast_to(
        sinks.astype(jnp.float32).reshape(N_KV_HEADS, GQA_GROUP)[:, :, None, None],
        s.shape[:-1] + (1,))
    p = jax.nn.softmax(jnp.concatenate([s, sink], axis=-1), axis=-1)[..., :-1]
    o = jnp.einsum('bnhgqk,bnkhd->bnqhgd', p.astype(v.dtype), vb)
    return o.reshape(B, S, N_Q_HEADS * HEAD_DIM) @ w_o

def spatial_gating_unit(h, w_in, v_gain, w_s, b_s, w_out):
    B, S, _ = h.shape
    z = jax.nn.gelu(h @ w_in, approximate=False)
    u, v = jnp.split(z, 2, axis=-1)
    v = _rms(v) * v_gain
    nS = S // SGU_CHUNK
    v = v.reshape(B, nS, SGU_CHUNK, SGU_GROUPS, SGU_GROUP_DIM)
    pos = np.arange(SGU_CHUNK) // CHUNK
    mask = jnp.asarray(pos[:, None] >= pos[None, :], dtype=w_s.dtype)
    w = w_s * mask
    sv = jnp.einsum('gts,bnsgd->bntgd', w, v) + jnp.transpose(b_s)[None, None, :, :, None]
    y = u * sv.reshape(B, S, SGU_WIDTH)
    return y @ w_out

def swiglu(h, w_gate, w_up, w_down):
    return (jax.nn.silu(h @ w_gate) * (h @ w_up)) @ w_down

def setup_inputs(seed: int = 0) -> dict:
    key = jax.random.key(seed)
    ks = jax.random.split(key, 20)
    f32 = jnp.float32
    D = D_MODEL
    T = SGU_CHUNK
    nrm = lambda k, shape, s: jax.random.normal(k, shape, f32) * s
    return {
        "x": nrm(ks[0], (BATCH, SEQ, D), 1.0),
        "c": nrm(ks[1], (BATCH, D), 1.0),
        "w_ada": nrm(ks[2], (DEPTH, D, N_MOD * D), 0.5 * D ** -0.5),
        "b_ada": nrm(ks[3], (DEPTH, N_MOD * D), 0.02),
        "attn_w_qkv": nrm(ks[4], (N_LAYERS_A, D, QKV_WIDTH), D ** -0.5),
        "attn_q_gain": 1.0 + nrm(ks[5], (N_LAYERS_A, HEAD_DIM), 0.05),
        "attn_k_gain": 1.0 + nrm(ks[6], (N_LAYERS_A, HEAD_DIM), 0.05),
        "attn_sinks": nrm(ks[7], (N_LAYERS_A, N_Q_HEADS), 0.5),
        "attn_w_o": nrm(ks[8], (N_LAYERS_A, N_Q_HEADS * HEAD_DIM, D), (N_Q_HEADS * HEAD_DIM) ** -0.5),
        "sgu_w_in": nrm(ks[9], (N_LAYERS_B, D, 2 * SGU_WIDTH), D ** -0.5),
        "sgu_v_gain": 1.0 + nrm(ks[10], (N_LAYERS_B, SGU_WIDTH), 0.05),
        "sgu_w_s": nrm(ks[11], (N_LAYERS_B, SGU_GROUPS, T, T), T ** -0.5),
        "sgu_b_s": 1.0 + nrm(ks[12], (N_LAYERS_B, SGU_GROUPS, T), 0.05),
        "sgu_w_out": nrm(ks[13], (N_LAYERS_B, SGU_WIDTH, D), SGU_WIDTH ** -0.5),
        "ffn_w_gate": nrm(ks[14], (DEPTH, D, D_FF), D ** -0.5),
        "ffn_w_up": nrm(ks[15], (DEPTH, D, D_FF), D ** -0.5),
        "ffn_w_down": nrm(ks[16], (DEPTH, D_FF, D), D_FF ** -0.5),
    }

def reference(x, c, w_ada, b_ada, attn_w_qkv, attn_q_gain, attn_k_gain, attn_sinks, attn_w_o,
              sgu_w_in, sgu_v_gain, sgu_w_s, sgu_b_s, sgu_w_out,
              ffn_w_gate, ffn_w_up, ffn_w_down):
    c_act = jax.nn.silu(c)
    for layer in range(DEPTH):
        mod = c_act @ w_ada[layer] + b_ada[layer]
        sh1, sc1, g1, sh2, sc2, g2 = jnp.split(mod, N_MOD, axis=-1)
        h = _modulate(x, sh1, sc1)
        j = layer // N_MIXERS
        if layer % N_MIXERS == 0:
            y = sliding_window_attention(h, attn_w_qkv[j], attn_q_gain[j], attn_k_gain[j],
                                         attn_sinks[j], attn_w_o[j])
        else:
            y = spatial_gating_unit(h, sgu_w_in[j], sgu_v_gain[j], sgu_w_s[j], sgu_b_s[j],
                                    sgu_w_out[j])
        x = x + g1[:, None, :] * y
        h = _modulate(x, sh2, sc2)
        x = x + g2[:, None, :] * swiglu(h, ffn_w_gate[layer], ffn_w_up[layer], ffn_w_down[layer])
    return x


_drawn_inputs = setup_inputs


def setup_inputs(seed=0):
    import zlib

    import numpy as np

    out = dict(_drawn_inputs(seed))
    spreads = {}
    factors = {'attn_q_gain': 8.0,
     'attn_k_gain': 8.0,
     'attn_sinks': 8.0,
     'sgu_v_gain': 6.197,
     'sgu_b_s': 5.385}
    for name, (base, spread) in spreads.items():
        noise = np.random.default_rng([zlib.crc32(name.encode()), seed]).standard_normal(out[name].shape)
        drawn = base * np.exp(spread * noise) if base else spread * noise
        out[name] = __import__('jax').numpy.asarray(drawn.astype(out[name].dtype))
    for name, factor in factors.items():
        out[name] = (out[name] * factor).astype(out[name].dtype)
    return out
```

```python
import math
from contextlib import ExitStack

import numpy as np

import concourse.bass as bass
from concourse import mybir
from concourse.alu_op_type import AluOpType as ALU

F32 = mybir.dt.float32
F32R = mybir.dt.float32r
ACT = mybir.ActivationFunctionType
AX = mybir.AxisListType

P = 128
D = 2048
S = 256
DT = D // P
FF = 5632
HEAD = 64
HEADS = D // HEAD
KV_HEADS = 4
PAIRS = HEADS // 2
NWIN = S // HEAD
GROUPS = 16
EPS = 1e-6
NMOD = 6
SH1, SC1, G1, SH2, SC2, G2 = range(NMOD)

RING = 4
KC = 4
NB = 512
BT = NB // P
SPLIT = 4
KU = 2
AHEAD = 4
ADA_BLOCKS = NMOD * D // NB
ADA_PER_VECTOR = D // NB
MOD_COLS = NMOD * D // P
PHASES = [4, 4, 3]

QKV_BLOCKS = (HEADS + 2 * KV_HEADS) * HEAD // NB
OUT_BLOCKS = D // NB

PRO_ITEMS = 2 * ADA_PER_VECTOR * 4


def weave(units, steps):
    done = [min(steps, steps * (u + 1) // (units - 2)) for u in range(units)]
    return [b - a for a, b in zip([0] + done, done)]


BODY_STEPS = [0, 0, 1, 1, 2, 1, 1, 2, 1, 1, 2, 1, 1, 2, 0, 0]
BODY_SUM_AFTER = 11


def ring_order(steps):
    order, taken = [], 0
    for u, n in enumerate(steps):
        if u % 2 == 0:
            order.append(("w", u // 2))
        for _ in range(n):
            if taken % KC == 0:
                order.append(("a", taken // KC))
            taken += 1
    return order


class Stretch:

    def __init__(self, before, units, steps, block_units, repeat=1):
        self.units, self.steps, self.repeat, self.block_units = units, steps, repeat, block_units
        self.order = ring_order(steps)
        self.per_body = len(self.order)
        self.ada_items = sum(steps) // KC
        self.item0, self.chunk0, self.block0, self.ada0 = before
        self.unit0 = 2 * self.chunk0
        self.end = (self.item0 + self.per_body * repeat, self.chunk0 + units // 2 * repeat,
                    self.block0 + units // block_units * repeat, self.ada0 + self.ada_items * repeat)

    def place(self, r, i=0):
        return (self.item0 + r) % RING, (self.item0 + r) // RING + 1 + (self.per_body // RING) * i

    def places(self, kind, i=0):
        return {n: self.place(r, i) for r, (k, n) in enumerate(self.order) if k == kind}

    def sums_after(self):
        done, found = 0, {}
        for u, n in enumerate(self.steps):
            for _ in range(n):
                done += 1
                if done % DT == 0:
                    found[max(u - 2, 0)] = done // DT - 1
        return found


def plan():
    attn = Stretch((PRO_ITEMS, 0, 0, PRO_ITEMS), 72, weave(72, 192), 8)
    at = attn.end
    ffns = []
    for layer in range(2):
        if layer:
            sgu = Stretch(at, 96, weave(96, 128), 8)
            at = sgu.end
        phases = []
        for ph, blocks in enumerate(PHASES):
            woven = layer == 0 or ph == 0
            up = Stretch(at, 16, BODY_STEPS if woven else [0] * 16, 8, blocks)
            n = 8 * blocks
            down = Stretch(up.end, n, weave(n, ([32, 32, 16] if layer == 0 else [0] * 3)[ph]), 2 * blocks)
            at = down.end
            phases.append((up, down))
        ffns.append(phases)
    return attn, ffns[0], sgu, ffns[1]


ATTN, FFN0, SGU, FFN1 = plan()
FFN = [FFN0, FFN1]
A_COUNT = [PAIRS, PAIRS + sum(PHASES) + 4]
A_SGU = PAIRS + sum(PHASES)
OUT_TURNS = [FFN1[2][1].block_units * (b + 1) + 2 for b in range(4)]
NORM_BLOCKS = [0, 4, 8, 16]


def trunk(nc, x_in, c_in, w_ada, b_ada, w_qkv, q_gain, k_gain, sinks, w_o, w_in, v_gain, w_s, b_s, w_out,
          w_gate, w_up, w_down, const_tiles, const_slopes, out):
    ctx = ExitStack()
    with ctx:
        def sb(name, shape, dt=F32):
            return ctx.enter_context(nc.sbuf_tensor(name, shape, dt))

        def sem(name):
            return ctx.enter_context(nc.semaphore(name))

        x = sb("x", [P, DT, S])
        h_hi = sb("h_hi", [P, DT, S], F32R)
        h_lo = sb("h_lo", [P, DT, S], F32R)
        a_hi = sb("a_hi", [P, DT, S], F32R)
        a_lo = sb("a_lo", [P, DT, S], F32R)
        ring = [sb(f"ring{s}", [P, KC, NB]) for s in range(RING)]
        w_hi = [sb(f"w_hi{s}", [P, KU, NB], F32R) for s in range(SPLIT)]
        w_lo = [sb(f"w_lo{s}", [P, KU, NB], F32R) for s in range(SPLIT)]
        ada = sb("ada", [P, 2, 2, NB])
        consts = sb("consts", [P, 5, P])
        ident, ones, head_ones, dist, mask = (consts[:, i, :] for i in range(5))
        slopes = sb("slopes", [P, PAIRS])
        sinkt = sb("sinkt", [P, PAIRS])
        mod = sb("mod", [P, 2 * MOD_COLS])
        bias_t = sb("bias_t", [P, 2 * MOD_COLS])
        c_act = sb("c_act", [P, DT])
        vgain = sb("vgain", [P, DT])
        gains = sb("gains", [P, 2])
        kgain = sb("kgain", [P, 1])
        epst = sb("epst", [P, 1])
        root = sb("root", [P, S])
        rstd = sb("rstd", [P, S])
        small = sb("small", [P, 80])
        qrstd, qroot, smax, den, inv = (small[:, a:b] for a, b in ((0, 16), (16, 32), (32, 36), (36, 40), (40, 44)))
        negmax, expsum, sinkexp = ([small[:, a + 4 * i:a + 4 * i + 4] for i in range(2)] for a in (44, 52, 60))
        vroot, vrstd = small[:, 68:70], small[:, 70:72]
        sink_row = sb("sink_row", [1, HEADS])
        work = sb("work", [P, 10752])

        def area(start, *shape):
            n = int(np.prod(shape))
            v = work[:, start:start + n]
            if len(shape) == 2:
                v = v.rearrange("p (a b) -> p a b", a=shape[0])
            if len(shape) == 3:
                v = v.rearrange("p (a b c) -> p a b c", a=shape[0], b=shape[1])
            return v

        x_tok = area(0, 2, D)
        rows = area(4096, 4, P)
        sq = area(4608, BT, S)
        parts = area(5632, BT, S)
        xr = [area(6656, BT, S), area(7680, BT, S)]
        hf = [area(8704, BT, S), area(9728, BT, S)]
        gate, hid = xr
        x_out = [area(0, 2, NB), area(1024, 2, NB)]
        qbd = area(0, PAIRS // KV_HEADS, NWIN, P)
        kdup = area(2048, KV_HEADS, S)
        vtok = area(3072, NWIN, S)
        pt = [area(4096 + 512 * i, NWIN, P) for i in range(2)]
        sc = [area(5120 + 512 * i, NWIN, P) for i in range(2)]
        pr = [area(6144 + 512 * i, NWIN, P) for i in range(2)]
        qsq = area(7168, BT, S)
        vpad = area(8192, 2, S + HEAD)
        kraw = area(8832, 2, S)
        ksq = area(9344, 2, S)
        abias = [area(9856 + P * i, P) for i in range(2)]
        krstd = area(10112, 512)
        vbuf = area(0, DT, S)
        bs_b = [area(4096, 4, P), area(10240, 4, P)]
        ugate, yf = xr
        ws_raw = [area(8704, 4, P), area(9216, 4, P)]
        ws_t = area(9728, 4, P)

        acc = ctx.enter_context(nc.psum_tensor("acc", [P, 2, BT, S], F32))
        aux = ctx.enter_context(nc.psum_tensor("aux", [P, 4, 512], F32))
        ADA_COLS = aux[:, 3, 0:2 * MOD_COLS]
        TURNED = aux[:, 1, 0:256]
        MIXED = aux[:, 0:2, :].rearrange("p b (t s) -> p (b t) s", t=2)
        VSTAT = aux[:, 2, 0:2]
        QSTAT = aux[:, 1, 0:16]

        consts_loaded = sem("consts_loaded")
        rows_loaded = sem("rows_loaded")
        x_loaded = sem("x_loaded")
        loaded = [sem(f"loaded{s}") for s in range(RING)]
        kdup_loaded = sem("kdup_loaded")
        ws_loaded = [sem("ws_loaded0"), sem("ws_loaded1")]
        out_stored = [sem("out_stored0"), sem("out_stored1")]
        hi_made = sem("hi_made")
        lo_made = sem("lo_made")
        units_done = sem("units_done")
        ada_steps = sem("ada_steps")
        ada_summed = sem("ada_summed")
        mod_made = sem("mod_made")
        acc_read = [sem("acc_read0"), sem("acc_read1")]
        eps_made = sem("eps_made")
        c_made = sem("c_made")
        vecs_loaded = sem("vecs_loaded")
        vecs_copied = sem("vecs_copied")
        bias_made = sem("bias_made")
        rows_turned = sem("rows_turned")
        kgain_made = sem("kgain_made")
        x_turned = sem("x_turned")
        x_copied = sem("x_copied")
        out_turned = sem("out_turned")
        out_copied = sem("out_copied")
        squared = sem("squared")
        parts_made = sem("parts_made")
        stat_summed = sem("stat_summed")
        root_made = sem("root_made")
        rstd_made = sem("rstd_made")
        xr_made = sem("xr_made")
        hf_made = sem("hf_made")
        h_hi_made = sem("h_hi_made")
        h_made = sem("h_made")
        att_cleared = sem("att_cleared")
        k_summed = sem("k_summed")
        k_root = sem("k_root")
        k_recip = sem("k_recip")
        k_normed = sem("k_normed")
        v_turned = sem("v_turned")
        v_copied = sem("v_copied")
        q_summed = sem("q_summed")
        q_root = sem("q_root")
        q_recip = sem("q_recip")
        abias_made = sem("abias_made")
        scored = sem("scored")
        biased = sem("biased")
        max_made = sem("max_made")
        negmax_made = sem("negmax_made")
        exp_made = sem("exp_made")
        den_made = sem("den_made")
        inv_made = sem("inv_made")
        probs_made = sem("probs_made")
        p_turned = sem("p_turned")
        p_copied = sem("p_copied")
        o_summed = sem("o_summed")
        y_made = sem("y_made")
        a_hi_made = sem("a_hi_made")
        a_made = sem("a_made")
        vstat_summed = sem("vstat_summed")
        vroot_made = sem("vroot_made")
        vrstd_made = sem("vrstd_made")
        ws_turned = sem("ws_turned")
        ws_masked = sem("ws_masked")
        vt_turned = sem("vt_turned")
        vt_copied = sem("vt_copied")
        mixed = sem("mixed")
        sv_made = sem("sv_made")

        block = ctx.enter_context(nc.Block())

        def mod_col(layer, m, tile):
            return layer * MOD_COLS + m * DT + tile

        def vector_made(layer, m):
            return (layer * NMOD + m + 1) * ADA_PER_VECTOR

        def rows_over(ap, n):
            return ap.unsqueeze(1).to_broadcast([P, n, ap.shape[1]])

        def v_tokens(k):
            return area(BT * S * k, 2, NB)


        @block.sync
        def _(sp):
            def groups_of(w):
                return w.rearrange("(g k p) n -> g p k n", k=KC, p=P)

            qkv_v, wo_v, win_v, wout_v = (groups_of(w[0]) for w in (w_qkv, w_o, w_in, w_out))
            gate_v, up_v, down_v = ([groups_of(w[l]) for l in range(2)] for w in (w_gate, w_up, w_down))
            ada_v = [groups_of(w_ada[l]) for l in range(2)]

            def columns(v, b):
                return v[:, :, bass.ds(NB * b, NB)]

            held = [None] * RING

            def send(slot, source, kind, number):
                if held[slot] is not None and held[slot][0] == "w":
                    sp.wait_ge(lo_made, 2 * held[slot][1] + 2)
                elif held[slot] is not None:
                    sp.wait_ge(ada_steps, KC * held[slot][1] + KC)
                sp.dma_start(ring[slot][:], source).then_inc(loaded[slot], 16)
                held[slot] = (kind, number)

            def send_body(st, chunk_source, i=0):
                q0 = st.ada0 // KC
                for r, (kind, n) in enumerate(st.order):
                    slot = st.place(r)[0]
                    if kind == "w":
                        send(slot, chunk_source(n, i), "w", st.chunk0 + st.units // 2 * i + n)
                    else:
                        layer, b = divmod(q0 + n // KC, ADA_BLOCKS)
                        send(slot, columns(ada_v[layer][n % KC], b + i), "a", st.ada0 + st.ada_items * i + n)

            sp.wait_ge(rows_loaded, 16)
            for n in range(PRO_ITEMS):
                send(n % RING, columns(ada_v[0][n % KC], n // KC), "a", n)

            def attn_chunk(n, i):
                b, k = divmod(n, 4)
                if b == 0:
                    return columns(qkv_v[k], QKV_BLOCKS - 1)
                return columns(qkv_v[k], b - 1) if b < QKV_BLOCKS else columns(wo_v[k], b - QKV_BLOCKS)

            def sgu_chunk(n, i):
                b, k = divmod(n, 4)
                if b < 2 * OUT_BLOCKS:
                    return columns(win_v[k], (b + OUT_BLOCKS) % (2 * OUT_BLOCKS))
                return columns(wout_v[k], b - 2 * OUT_BLOCKS)

            def send_ffn(layer):
                for ph, (up, down) in enumerate(FFN[layer]):
                    def up_chunk(n, i):
                        return columns((gate_v, up_v)[n // 4][layer][n % 4], PHASES[0] * ph + i)

                    def down_chunk(n, i):
                        b, k = divmod(n, PHASES[ph])
                        return columns(down_v[layer][PHASES[0] * ph + k], b)

                    send_body(up, up_chunk)
                    first = list(held)
                    body_of = {"w": up.units // 2, "a": up.ada_items}
                    with sp.Fori(1, up.repeat) as i:
                        held[:] = [(kind, n + body_of[kind] * (i - 1)) for kind, n in first]
                        send_body(up, up_chunk, i)
                    held[:] = [(kind, n + body_of[kind] * (up.repeat - 1)) for kind, n in first]
                    send_body(down, down_chunk)

            send_body(ATTN, attn_chunk)
            send_ffn(0)
            send_body(SGU, sgu_chunk)
            send_ffn(1)

            out_v = out[0].rearrange("(b p) n -> p b n", p=P)
            for b in range(OUT_BLOCKS):
                sp.wait_ge(out_copied, b + 1)
                sp.dma_start(out_v[:, :, NB * b:NB * (b + 1)], x_out[b % 2]).then_inc(out_stored[b % 2], 16)
            for s in range(2):
                sp.wait_ge(out_stored[s], 16 * (OUT_BLOCKS // 2))

        @block.gpsimd
        def _(pool):
            nc.gpsimd.memset(epst[:], EPS).then_inc(eps_made, 1)
            pool.wait_ge(h_made, 4)
            nc.gpsimd.memset(qbd, 0.0)
            nc.gpsimd.memset(vpad[:, :, 0:HEAD], 0.0)
            for i in range(2):
                nc.gpsimd.memset(sc[i][:, 0, 0:HEAD], -1e30)
                last = nc.gpsimd.memset(pr[i][:, 0, 0:HEAD], 0.0)
            last.then_inc(att_cleared, 1)
            pool.wait_ge(k_normed, 1)
            kd = kdup.rearrange("p (m two) s -> p two m s", two=2)
            for half in range(2):
                for to in range(2):
                    pool.dma_start(kd[HEAD * to:HEAD * to + HEAD, half], kraw[HEAD * half:HEAD * half + HEAD])\
                        .then_inc(kdup_loaded, 16)
            ws_v = w_s[0].rearrange("(k g) t s -> k t g s", g=4)
            bs_v = b_s[0].rearrange("(k g) t -> k (g t)", g=4)
            pool.wait_ge(h_made, 12)
            for k in range(4):
                if k >= 2:
                    pool.wait_ge(ws_turned, k - 1)
                    pool.wait_ge(sv_made, k - 1)
                pool.dma_start(ws_raw[k % 2], ws_v[k]).then_inc(ws_loaded[k % 2], 16)
                pool.dma_start(bs_b[k % 2].rearrange("p g t -> p (g t)"), bs_v[k].partition_broadcast(P))\
                    .then_inc(ws_loaded[k % 2], 16)

        @block.scalar
        def _(act):
            act.dma_start(rows[0:DT, 0, :], c_in.rearrange("b (t p) -> (b t) p", p=P)).then_inc(rows_loaded, 16)
            act.dma_start(consts[:], const_tiles).then_inc(consts_loaded, 16)
            act.dma_start(x_tok, x_in[0].rearrange("(b p) n -> p b n", p=P)).then_inc(x_loaded, 16)
            act.dma_start(rows[0:DT, 1, :], v_gain.rearrange("b (t p) -> (b t) p", p=P)).then_inc(vecs_loaded, 16)
            for l in range(2):
                act.dma_start(rows[0:MOD_COLS, 2 + l, :], b_ada[l].rearrange("(t p) -> t p", p=P))\
                    .then_inc(vecs_loaded, 16)
            act.dma_start(slopes[:], const_slopes).then_inc(vecs_loaded, 16)
            act.dma_start(sink_row[:], sinks).then_inc(vecs_loaded, 16)
            for half in range(2):
                for i, g in enumerate((q_gain, k_gain)):
                    act.dma_start(gains[HEAD * half:HEAD * half + HEAD, i:i + 1], g.rearrange("a d -> d a"))\
                        .then_inc(vecs_loaded, 16)

            act.wait_ge(rows_turned, 1)
            nc.scalar.activation(c_act[:], TURNED[:, 0:DT], ACT.Silu).then_inc(c_made, 1)

            def square_block(n, source):
                if n:
                    act.wait_ge(parts_made, n)
                nc.scalar.activation(sq, source, ACT.Square).then_inc(squared, 1)

            def square_x(sub, b):
                square_block(NORM_BLOCKS[sub] + b, x[:, 4 * b:4 * b + 4, :])

            for b in range(4):
                act.wait_ge(x_turned, b + 1)
                nc.scalar.copy(x[:, 4 * b:4 * b + 4, :], acc[:, b % 2]).then_inc(x_copied, 1)

            act.wait_ge(rows_turned, 2)
            nc.scalar.copy(vgain[:], TURNED[:, DT:2 * DT])
            nc.scalar.copy(bias_t[:], TURNED[:, 2 * DT:2 * DT + 2 * MOD_COLS])
            nc.scalar.copy(sinkt[:], TURNED[:, 240:240 + PAIRS]).then_inc(vecs_copied, 1)

            for b in range(4):
                act.wait_ge(x_copied, b + 1)
                square_x(0, b)

            def norm_root(sub):
                act.wait_ge(stat_summed, sub + 1)
                act.wait_ge(eps_made, 1)
                nc.scalar.activation(root[:], aux[:, 2, 0:S], ACT.Sqrt, bias=epst[:], scale=1.0 / D)\
                    .then_inc(root_made, 1)

            def modulate(sub, g):
                layer, n = sub // 2, 4 * sub + g
                scale, shift = (mod_col(layer, m, 4 * g) for m in ((SC1, SC2)[sub % 2], (SH1, SH2)[sub % 2]))
                act.wait_ge(xr_made, n + 1)
                act.wait_ge(mod_made, vector_made(layer, (SC1, SC2)[sub % 2]))
                if g >= 2:
                    act.wait_ge(h_made, n - 1)
                for t in range(BT):
                    last = nc.scalar.activation(hf[g % 2][:, t, :], xr[g % 2][:, t, :], ACT.Identity,
                                                bias=mod[:, shift + t:shift + t + 1],
                                                scale=mod[:, scale + t:scale + t + 1])
                last.then_inc(hf_made, 1)
                act.wait_ge(hf_made, n + 1)
                nc.scalar.copy(h_hi[:, 4 * g:4 * g + 4, :], hf[g % 2]).then_inc(h_hi_made, 1)

            def start_norm(sub):
                norm_root(sub)
                modulate(sub, 0)
                modulate(sub, 1)

            def split_hi(st, u, i=0):
                slot, round_ = st.places("w", i)[u // 2]
                unit = st.unit0 + st.units * i + u
                act.wait_ge(loaded[slot], 16 * round_)
                if st.unit0 + u >= SPLIT:
                    act.wait_ge(units_done, unit + 1 - SPLIT)
                nc.scalar.copy(w_hi[u % SPLIT][:], ring[slot][:, KU * (u % 2):KU * (u % 2) + KU, :])\
                    .then_inc(hi_made, 1)

            def split_stretch(st, after_last, after_unit, i=0):
                for u in range(st.units):
                    if u == AHEAD - 1:
                        after_last()
                    if u >= AHEAD:
                        after_unit(u - AHEAD)
                    split_hi(st, u, i)

            def with_norm(sub, after_unit):
                def after(u):
                    if u in (0, 2):
                        modulate(sub, 2 + u // 2)
                    after_unit(u)
                return after

            def read_kv():
                act.wait_ge(units_done, 8)
                act.wait_ge(att_cleared, 1)
                nc.scalar.copy(kraw, acc[:, 0, 0:2, :])
                nc.scalar.activation(ksq, acc[:, 0, 0:2, :], ACT.Square)
                nc.scalar.copy(vpad[:, :, HEAD:], acc[:, 0, 2:4, :]).then_inc(acc_read[0], 1)

            def read_q(g):
                b = 1 + g
                act.wait_ge(units_done, 8 * (b + 1))
                act.wait_ge(att_cleared, 1)
                if g:
                    act.wait_ge(scored, 4 * g)
                for half in range(2):
                    hp = slice(HEAD * half, HEAD * half + HEAD)
                    nc.scalar.copy(qbd[hp, :, :, HEAD * half:HEAD * half + HEAD].rearrange("p t n q -> p (t n) q"),
                                   acc[hp, b % 2].rearrange("p t (n q) -> p (t n) q", q=HEAD))
                nc.scalar.activation(qsq, acc[:, b % 2], ACT.Square).then_inc(acc_read[b % 2], 1)

            def bias_of(j):
                if j >= 2:
                    act.wait_ge(biased, j - 1)
                nc.scalar.activation(abias[j % 2], dist, ACT.Copy, scale=slopes[:, j:j + 1]).then_inc(abias_made, 1)

            def exps(j):
                act.wait_ge(negmax_made, j + 1)
                if j >= 2:
                    act.wait_ge(p_turned, j - 1)
                for n in range(NWIN):
                    k0 = HEAD if n == 0 else 0
                    nc.scalar.activation(pr[j % 2][:, n, k0:], sc[j % 2][:, n, k0:], ACT.Exp,
                                         bias=negmax[j % 2][:, n:n + 1], accum_out=expsum[j % 2][:, n:n + 1])
                nc.scalar.activation(sinkexp[j % 2], negmax[j % 2], ACT.Exp, bias=sinkt[:, j:j + 1])\
                    .then_inc(exp_made, 1)

            def copy_turned(j):
                act.wait_ge(p_turned, j + 1)
                if j >= 2:
                    act.wait_ge(o_summed, j - 1)
                nc.scalar.copy(pt[j % 2], aux[:, 1, :].rearrange("p (n q) -> p n q", n=NWIN)).then_inc(p_copied, 1)

            def o_hi(j):
                act.wait_ge(o_summed, j + 1)
                nc.scalar.copy(a_hi[:, j, :], aux[:, 2, S * (j % 2):S * (j % 2) + S]).then_inc(a_hi_made, 1)

            def after_out(b, block, sub):
                act.wait_ge(acc_read[block % 2], block // 2 + 1)
                square_x(sub, b)

            def attn_after(u):
                b, s = divmod(u, 8)
                if s == 7:
                    if b == 0:
                        read_kv()
                    elif b < QKV_BLOCKS:
                        read_q(b - 1)
                    else:
                        after_out(b - QKV_BLOCKS, b, 1)
                if b == 1 and s == 1:
                    act.wait_ge(k_summed, 1)
                    nc.scalar.activation(krstd, aux[:, 0, :], ACT.Sqrt, bias=epst[:], scale=1.0 / HEAD)\
                        .then_inc(k_root, 1)
                if b == 1 and s in (2, 3):
                    act.wait_ge(v_turned, s - 1)
                    nc.scalar.copy(vtok[:, 2 * (s - 2):2 * (s - 2) + 2, :],
                                   aux[:, 1, :].rearrange("p (n d) -> p n d", n=2)).then_inc(v_copied, 1)
                if 2 <= b < 2 + KV_HEADS:
                    g, j = b - 2, 4 * (b - 2)
                    if s == 1:
                        act.wait_ge(q_summed, g + 1)
                        nc.scalar.activation(qroot, QSTAT, ACT.Sqrt, bias=epst[:], scale=1.0 / HEAD)\
                            .then_inc(q_root, 1)
                        bias_of(j)
                        bias_of(j + 1)
                        exps(j)
                    if s == 2:
                        bias_of(j + 2)
                        exps(j + 1)
                    if s == 3:
                        bias_of(j + 3)
                        copy_turned(j)
                        exps(j + 2)
                    if s == 4:
                        copy_turned(j + 1)
                        exps(j + 3)
                        o_hi(j)
                    if s == 5:
                        o_hi(j + 1)
                        copy_turned(j + 2)
                        o_hi(j + 2)
                        copy_turned(j + 3)
                        o_hi(j + 3)

            split_stretch(ATTN, lambda: start_norm(0), with_norm(0, attn_after))

            def ffn(layer, start):
                sub, a0 = 2 * layer + 1, A_COUNT[layer]
                after_last = start
                for ph, (up, down) in enumerate(FFN[layer]):
                    gp, upp = up.block0 % 2, (up.block0 + 1) % 2

                    def after_up(i):
                        act.wait_ge(acc_read[upp], (up.block0 + 1) // 2 + 1 + i)
                        nc.scalar.copy(a_hi[:, bass.ds(4 * i, 4), :], hid).then_inc(a_hi_made, 1)

                    def after_gate(i):
                        act.wait_ge(units_done, up.unit0 + up.units * i + 8)
                        act.wait_ge(acc_read[upp], (up.block0 + 1) // 2 + i)
                        nc.scalar.activation(gate, acc[:, gp], ACT.Silu).then_inc(acc_read[gp], 1)

                    def body(i, after_last, norm):
                        def after_unit(u):
                            if u == 7:
                                after_gate(i)
                        split_stretch(up, after_last, with_norm(sub, after_unit) if norm else after_unit, i)

                    body(0, after_last, ph == 0)
                    with act.Fori(1, up.repeat) as i:
                        body(i, lambda: after_up(i - 1), False)

                    def after_down(u):
                        b, s = divmod(u, down.block_units)
                        if ph == 2 and s == down.block_units - 1 and layer == 0:
                            after_out(b, down.block0 + b, 2)
                        if ph == 2 and layer == 1 and u in OUT_TURNS:
                            store_block(OUT_TURNS.index(u))

                    split_stretch(down, lambda: after_up(up.repeat - 1), after_down)
                    after_last = lambda: None

            def store_block(b):
                act.wait_ge(out_turned, b + 1)
                if b >= 2:
                    act.wait_ge(out_stored[b % 2], 16)
                nc.scalar.copy(x_out[b % 2], aux[:, 0:2, :]).then_inc(out_copied, 1)

            def next_norm(sub, last_block):
                def f():
                    after_out(3, last_block, sub)
                    start_norm(sub)
                return f

            ffn(0, next_norm(1, ATTN.end[2] - 1))

            def sgu_after(u):
                b, s = divmod(u, 8)
                block = SGU.block0 + b
                par = block % 2
                if s == 7 and b < 4:
                    act.wait_ge(units_done, SGU.unit0 + u + 1)
                    nc.scalar.activation(vbuf[:, 4 * b:4 * b + 4, :], acc[:, par], ACT.Gelu).then_inc(acc_read[par], 1)
                    act.wait_ge(acc_read[par], block // 2 + 1)
                    square_block(12 + b, vbuf[:, 4 * b:4 * b + 4, :])
                elif s == 7 and b < 8:
                    act.wait_ge(units_done, SGU.unit0 + u + 1)
                    if b > 4:
                        act.wait_ge(y_made, b - 4)
                    nc.scalar.activation(ugate, acc[:, par], ACT.Gelu).then_inc(acc_read[par], 1)
                    act.wait_ge(y_made, b - 3)
                    nc.scalar.copy(a_hi[:, 4 * (b - 4):4 * (b - 4) + 4, :], yf).then_inc(a_hi_made, 1)
                elif s == 7:
                    after_out(b - 8, block, 3)
                if u == 32:
                    act.wait_ge(vstat_summed, 1)
                    nc.scalar.activation(vroot, VSTAT, ACT.Sqrt, bias=epst[:], scale=1.0 / D).then_inc(vroot_made, 1)
                if 33 <= u < 41 and u % 2 == 1:
                    k = (u - 33) // 2
                    act.wait_ge(vrstd_made, 1)
                    act.wait_ge(vt_turned, k + 1)
                    for n in range(2):
                        last = nc.scalar.activation(v_tokens(k)[:, n, :], aux[:, n, :], ACT.Copy,
                                                    scale=vrstd[:, n:n + 1])
                    last.then_inc(vt_copied, 1)

            split_stretch(SGU, next_norm(2, FFN0[2][1].end[2] - 1), with_norm(2, sgu_after))
            ffn(1, next_norm(3, SGU.end[2] - 1))
            for b in range(OUT_BLOCKS):
                if OUT_TURNS[b] >= FFN1[2][1].units - AHEAD:
                    store_block(b)

        @block.vector
        def _(dve):
            def reduce_block(n, read_by, times):
                dve.wait_ge(squared, n + 1)
                if times:
                    dve.wait_ge(read_by, times)
                nc.vector.tensor_reduce(out=parts[:, n % 4, :], in_=sq.rearrange("p t s -> p s t"), axis=AX.X,
                                        op=ALU.add).then_inc(parts_made, 1)

            def reduce_x(sub, b):
                reduce_block(NORM_BLOCKS[sub] + b, *((vstat_summed, 1) if sub == 3 else (stat_summed, sub)))

            def ada_step(q, s, slot, round_, looped, after_loop, i=0):
                parts_n = 1 if looped else 2
                buf = 0 if looped else q % 2
                into = ada[:, buf, s % parts_n, :]
                if s % KC == 0:
                    dve.wait_ge(loaded[slot], 16 * round_)
                weight, scale = ring[slot][:, s % KC, :], c_act[:, s:s + 1]
                if s < parts_n:
                    if looped or after_loop or q >= 2:
                        dve.wait_ge(ada_summed, q + i - (0 if looped or after_loop else 1))
                    nc.vector.tensor_scalar(into, weight, scale, None, ALU.mult).then_inc(ada_steps, 1)
                else:
                    dve.wait_ge(ada_steps, DT * (q + i) + s - parts_n + 1)
                    nc.vector.scalar_tensor_tensor(out=into, in0=weight, scalar=scale, in1=into,
                                                   op0=ALU.mult, op1=ALU.add).then_inc(ada_steps, 1)

            def make_mod(q, i=0):
                cols = bass.ds(BT * q + BT * i, BT)
                dve.wait_ge(ada_summed, q + i + 1)
                nc.vector.tensor_tensor(mod[:, cols], ADA_COLS[:, cols], bias_t[:, cols], ALU.add)\
                    .then_inc(mod_made, 1)

            def update_x(layer, m, b, block, end_unit):
                g = mod_col(layer, m, 4 * b)
                dve.wait_ge(units_done, end_unit)
                dve.wait_ge(mod_made, vector_made(layer, m))
                for t in range(BT):
                    xt = x[:, 4 * b + t, :]
                    last = nc.vector.scalar_tensor_tensor(out=xt, in0=acc[:, block % 2, t, :],
                                                          scalar=mod[:, g + t:g + t + 1], in1=xt,
                                                          op0=ALU.mult, op1=ALU.add)
                last.then_inc(acc_read[block % 2], 1)

            def norm_x(sub, g):
                if g == 0:
                    dve.wait_ge(root_made, sub + 1)
                    nc.vector.reciprocal(rstd[:], root[:]).then_inc(rstd_made, 1)
                    dve.wait_ge(rstd_made, sub + 1)
                if g >= 2:
                    dve.wait_ge(h_hi_made, 4 * sub + g - 1)
                nc.vector.tensor_tensor(xr[g % 2], x[:, 4 * g:4 * g + 4, :], rows_over(rstd[:], BT), ALU.mult)\
                    .then_inc(xr_made, 1)

            def h_lo_of(sub, g):
                n = 4 * sub + g
                dve.wait_ge(h_hi_made, n + 1)
                nc.vector.tensor_tensor(h_lo[:, 4 * g:4 * g + 4, :], hf[g % 2],
                                        h_hi[:, 4 * g:4 * g + 4, :].bitcast(F32), ALU.subtract).then_inc(h_made, 1)

            def start_norm(sub):
                norm_x(sub, 0)
                norm_x(sub, 1)
                h_lo_of(sub, 0)
                norm_x(sub, 2)
                h_lo_of(sub, 1)

            def with_norm(sub, after_unit):
                def after(u):
                    if u == 0:
                        norm_x(sub, 3)
                        h_lo_of(sub, 2)
                    if u == 2:
                        h_lo_of(sub, 3)
                    after_unit(u)
                return after

            def split_lo(st, u, i=0):
                slot = st.places("w")[u // 2][0]
                dve.wait_ge(hi_made, st.unit0 + st.units * i + u + 1)
                nc.vector.tensor_tensor(w_lo[u % SPLIT][:], ring[slot][:, KU * (u % 2):KU * (u % 2) + KU, :],
                                        w_hi[u % SPLIT][:].bitcast(F32), ALU.subtract).then_inc(lo_made, 1)

            def split_stretch(st, after_last, after_unit, i=0, looped=False, after_loop=False):
                step, sums = 0, st.sums_after()
                if looped:
                    sums = {BODY_SUM_AFTER: 0} if st.ada_items else {}
                for u in range(st.units):
                    if u == AHEAD - 1:
                        after_last()
                    if u >= AHEAD:
                        after_unit(u - AHEAD)
                    if u - AHEAD in sums:
                        make_mod(st.ada0 // KC + sums[u - AHEAD], i)
                    split_lo(st, u, i)
                    for _ in range(st.steps[u]):
                        q, s = divmod(step, DT)
                        ada_step(st.ada0 // KC + q, s, *st.places("a", i)[step // KC], looped,
                                 after_loop and q == 0, i)
                        step += 1

            for q in range(PRO_ITEMS // KC):
                for s in range(DT):
                    if q == 0 and s == 0:
                        dve.wait_ge(c_made, 1)
                    n = KC * q + s // KC
                    ada_step(q, s, n % RING, n // RING + 1, False, False)
                if q == 1:
                    dve.wait_ge(vecs_copied, 1)
                    scale_bias = bias_t[:].rearrange("p (l h m t) -> p (l h) m t", l=2, h=2, t=DT)[:, :, SC1, :]
                    nc.vector.tensor_scalar(scale_bias, scale_bias, 1.0, None, ALU.add).then_inc(bias_made, 1)
                    dve.wait_ge(bias_made, 1)
                if q:
                    make_mod(q - 1)
                if q >= 4:
                    reduce_x(0, q - 4)
            make_mod(PRO_ITEMS // KC - 1)

            def norm_k():
                dve.wait_ge(vecs_loaded, 16 * 9)
                nc.vector.scalar_tensor_tensor(out=kgain[:], in0=gains[:, 0:1], scalar=HEAD ** -0.5,
                                               in1=gains[:, 1:2], op0=ALU.mult, op1=ALU.mult).then_inc(kgain_made, 1)
                dve.wait_ge(k_root, 1)
                nc.vector.reciprocal(krstd, krstd).then_inc(k_recip, 1)
                dve.wait_ge(k_recip, 1)
                dve.wait_ge(kgain_made, 1)
                kf = kraw.rearrange("p m s -> p (m s)")
                nc.vector.scalar_tensor_tensor(out=kf, in0=kf, scalar=kgain[:], in1=krstd,
                                               op0=ALU.mult, op1=ALU.mult).then_inc(k_normed, 1)

            def softmax_in(j):
                t, n_pairs = j % 4, PAIRS // KV_HEADS
                dve.wait_ge(scored, j + 1)
                dve.wait_ge(abias_made, j + 1)
                if j >= 2:
                    dve.wait_ge(exp_made, j - 1)
                for n in range(NWIN):
                    k0 = HEAD if n == 0 else 0
                    last = nc.vector.scalar_tensor_tensor(
                        out=sc[j % 2][:, n, k0:], in0=aux[:, 0, P * n + k0:P * n + P],
                        scalar=qrstd[:, n_pairs * t + n:n_pairs * t + n + 1], in1=abias[j % 2][:, k0:],
                        op0=ALU.mult, op1=ALU.add)
                last.then_inc(biased, 1)
                dve.wait_ge(biased, j + 1)
                nc.vector.tensor_reduce(out=smax, in_=sc[j % 2], axis=AX.X, op=ALU.max).then_inc(max_made, 1)
                dve.wait_ge(max_made, j + 1)
                nc.vector.tensor_scalar(negmax[j % 2], smax, sinkt[:, j:j + 1], -1.0, ALU.max, ALU.mult)\
                    .then_inc(negmax_made, 1)

            def softmax_out(j):
                dve.wait_ge(exp_made, j + 1)
                nc.vector.tensor_tensor(den, expsum[j % 2], sinkexp[j % 2], ALU.add).then_inc(den_made, 1)
                dve.wait_ge(den_made, j + 1)
                nc.vector.reciprocal(inv, den).then_inc(inv_made, 1)
                dve.wait_ge(inv_made, j + 1)
                nc.vector.tensor_tensor(pr[j % 2], pr[j % 2], inv.unsqueeze(2).to_broadcast([P, NWIN, P]), ALU.mult)\
                    .then_inc(probs_made, 1)

            def o_lo(j):
                dve.wait_ge(a_hi_made, j + 1)
                nc.vector.tensor_tensor(a_lo[:, j, :], aux[:, 2, S * (j % 2):S * (j % 2) + S],
                                        a_hi[:, j, :].bitcast(F32), ALU.subtract).then_inc(a_made, 1)

            def after_out(layer, m, b, block, end_unit, sub):
                update_x(layer, m, b, block, end_unit)
                reduce_x(sub, b)

            def attn_after(u):
                b, s = divmod(u, 8)
                if s == 7 and b >= QKV_BLOCKS:
                    after_out(0, G1, b - QKV_BLOCKS, b, u + 1, 1)
                if b == 1 and s == 1:
                    norm_k()
                if 2 <= b < 2 + KV_HEADS:
                    g, j = b - 2, 4 * (b - 2)
                    if s == 1:
                        dve.wait_ge(q_root, g + 1)
                        nc.vector.reciprocal(qrstd, qroot).then_inc(q_recip, 1)
                        dve.wait_ge(q_recip, g + 1)
                        softmax_in(j)
                    if s in (2, 3, 4):
                        softmax_out(j + s - 2)
                        softmax_in(j + s - 1)
                    if s == 4:
                        o_lo(j)
                    if s == 5:
                        softmax_out(j + 3)
                        for k in range(1, 4):
                            o_lo(j + k)

            split_stretch(ATTN, lambda: start_norm(0), with_norm(0, attn_after))

            def ffn(layer, start):
                sub, a0 = 2 * layer + 1, A_COUNT[layer]
                after_last = start
                done = 0
                for ph, (up, down) in enumerate(FFN[layer]):
                    gp, upp = up.block0 % 2, (up.block0 + 1) % 2

                    def multiply_up(i):
                        dve.wait_ge(units_done, up.unit0 + up.units * (i + 1))
                        dve.wait_ge(acc_read[gp], up.block0 // 2 + 1 + i)
                        nc.vector.tensor_tensor(hid, acc[:, upp], gate, ALU.mult).then_inc(acc_read[upp], 1)

                    def hidden_lo(i):
                        dve.wait_ge(a_hi_made, a0 + done + i + 1)
                        nc.vector.tensor_tensor(a_lo[:, bass.ds(4 * i, 4), :], hid,
                                                a_hi[:, bass.ds(4 * i, 4), :].bitcast(F32), ALU.subtract)\
                            .then_inc(a_made, 1)

                    def body(i, after_last, norm, previous=None):
                        def after_unit(u):
                            if u == 0 and previous is not None:
                                hidden_lo(previous)
                        split_stretch(up, after_last, with_norm(sub, after_unit) if norm else after_unit, i,
                                      looped=True)

                    body(0, after_last, ph == 0)
                    with dve.Fori(1, up.repeat) as i:
                        body(i, lambda: multiply_up(i - 1), False, i - 1)

                    def after_block(b, down=down, ph=ph):
                        end = down.unit0 + down.block_units * (b + 1)
                        if ph == 2 and layer == 0:
                            after_out(layer, G2, b, down.block0 + b, end, 2)
                        else:
                            update_x(layer, G2, b, down.block0 + b, end)

                    def after_down(u):
                        if u == 0:
                            hidden_lo(up.repeat - 1)
                        if (u + 1) % down.block_units == 0:
                            after_block(u // down.block_units)

                    split_stretch(down, lambda: multiply_up(up.repeat - 1), after_down, after_loop=True)
                    done += up.repeat
                    after_last = lambda after_block=after_block: after_block(3)
                    yield_last = after_last
                return yield_last

            def next_norm(sub, last):
                def f():
                    last()
                    start_norm(sub)
                return f

            last = ffn(0, next_norm(1, lambda: after_out(
                0, G1, 3, ATTN.end[2] - 1, ATTN.units, 1)))

            def sgu_after(u):
                b, s = divmod(u, 8)
                block = SGU.block0 + b
                if s == 7 and b < 4:
                    reduce_block(12 + b, stat_summed, 3)
                elif s == 7 and b < 8:
                    dve.wait_ge(acc_read[block % 2], block // 2 + 1)
                    dve.wait_ge(sv_made, b - 3)
                    nc.vector.tensor_tensor(yf, ugate, vbuf[:, 4 * (b - 4):4 * (b - 4) + 4, :], ALU.mult)\
                        .then_inc(y_made, 1)
                    dve.wait_ge(a_hi_made, A_SGU + b - 3)
                    nc.vector.tensor_tensor(a_lo[:, 4 * (b - 4):4 * (b - 4) + 4, :], yf,
                                            a_hi[:, 4 * (b - 4):4 * (b - 4) + 4, :].bitcast(F32), ALU.subtract)\
                        .then_inc(a_made, 1)
                elif s == 7:
                    after_out(1, G1, b - 8, block, SGU.unit0 + u + 1, 3)
                if u == 32:
                    dve.wait_ge(vroot_made, 1)
                    nc.vector.reciprocal(vrstd, vroot).then_inc(vrstd_made, 1)
                if 33 <= u < 41 and u % 2 == 1:
                    k = (u - 33) // 2
                    dve.wait_ge(ws_turned, k + 1)
                    if k:
                        dve.wait_ge(mixed, k)
                    nc.vector.tensor_tensor(ws_t, aux[:, 2, :].rearrange("p (g t) -> p g t", g=4),
                                            rows_over(mask, 4), ALU.mult).then_inc(ws_masked, 1)
                if 33 <= u < 41 and u % 2 == 0:
                    k = (u - 34) // 2
                    dve.wait_ge(mixed, k + 1)
                    dve.wait_ge(ws_loaded[k % 2], 32 * (k // 2 + 1))
                    for t in range(4):
                        last = nc.vector.scalar_tensor_tensor(
                            out=vbuf[:, 4 * k + t, :].rearrange("p (n t) -> p n t", n=2),
                            in0=MIXED[:, t, :].rearrange("p (n t) -> p n t", n=2),
                            scalar=vgain[:, 4 * k + t:4 * k + t + 1], in1=rows_over(bs_b[k % 2][:, t, :], 2),
                            op0=ALU.mult, op1=ALU.add)
                    last.then_inc(sv_made, 1)

            split_stretch(SGU, next_norm(2, last),
                          with_norm(2, sgu_after), after_loop=True)
            last = ffn(1, next_norm(3, lambda: after_out(
                1, G1, 3, SGU.end[2] - 1, 2 * SGU.end[1], 3)))
            last()

        @block.tensor
        def _(pe):
            def unit(st, u, act_hi, act_lo, kt, first, last_, par, i=0):
                pe.wait_ge(lo_made, st.unit0 + st.units * i + u + 1)
                hi, lo = w_hi[u % SPLIT], w_lo[u % SPLIT]
                for k in range(KU):
                    for t in range(BT):
                        cols, sums = slice(P * t, P * t + P), acc[:, par, t, :]
                        start = first and k == 0 and t % 2 == 0
                        stop = last_ and k == KU - 1
                        nc.tensor.matmul(sums, hi[:, k, cols], act_hi[:, kt + k, :], start=start, stop=False,
                                         skip_group_check=True)
                        nc.tensor.matmul(sums, hi[:, k, cols], act_lo[:, kt + k, :], start=False, stop=False,
                                         skip_group_check=True)
                        done = nc.tensor.matmul(sums, lo[:, k, cols], act_hi[:, kt + k, :], start=False, stop=stop,
                                                skip_group_check=True)
                done.then_inc(units_done, 1)

            def wait_sums_free(block, i=0):
                if block < 2:
                    pe.wait_ge(x_copied, 4)
                else:
                    pe.wait_ge(acc_read[block % 2], block // 2 + i)

            def ada_sum(q, looped, i=0):
                parts_n, buf = (1, 0) if looped else (2, q % 2)
                pe.wait_ge(ada_steps, DT * (q + i + 1))
                if looped or q:
                    pe.wait_ge(mod_made, q + i)
                for t in range(BT):
                    for part in range(parts_n):
                        done = nc.tensor.matmul(ADA_COLS[:, bass.ds(BT * q + BT * i + t, 1)],
                                                ada[:, buf, part, P * t:P * t + P], ones[:, 0:1],
                                                start=part == 0, stop=part == parts_n - 1, skip_group_check=True)
                done.then_inc(ada_summed, 1)

            def norm_stat(sub):
                pe.wait_ge(parts_made, NORM_BLOCKS[sub] + 4)
                for b in range(4):
                    done = nc.tensor.matmul(aux[:, 2, 0:S], ones, parts[:, b, :], start=b == 0, stop=b == 3)
                done.then_inc(stat_summed, 1)

            pe.wait_ge(consts_loaded, 16)
            pe.wait_ge(rows_loaded, 16)
            nc.tensor.transpose(TURNED[:, 0:DT], rows[0:DT, 0, :], ident[0:DT, 0:DT]).then_inc(rows_turned, 1)
            pe.wait_ge(x_loaded, 16)
            for b in range(4):
                if b >= 2:
                    pe.wait_ge(x_copied, b - 1)
                for n in range(2):
                    for t in range(4):
                        done = nc.tensor.transpose(acc[:, b % 2, t, P * n:P * n + P],
                                                   x_tok[:, n, P * (4 * b + t):P * (4 * b + t) + P], ident)
                done.then_inc(x_turned, 1)
            pe.wait_ge(vecs_loaded, 16 * 9)
            pe.wait_ge(c_made, 1)
            nc.tensor.transpose(TURNED[:, DT:2 * DT], rows[0:DT, 1, :], ident[0:DT, 0:DT])
            for l in range(2):
                nc.tensor.transpose(TURNED[:, 2 * DT + MOD_COLS * l:2 * DT + MOD_COLS * (l + 1)],
                                    rows[0:MOD_COLS, 2 + l, :], ident[0:MOD_COLS, 0:MOD_COLS])
            for half in range(2):
                done = nc.tensor.matmul(TURNED[HEAD * half:HEAD * half + HEAD, 240:240 + PAIRS], ones[0:1, 0:HEAD],
                                        sink_row[0:1, half:HEADS:2], start=True, stop=True)
            done.then_inc(rows_turned, 1)
            for q in range(PRO_ITEMS // KC):
                ada_sum(q, False)
            norm_stat(0)

            def turn_v(r):
                if r:
                    pe.wait_ge(v_copied, r)
                for n in range(2):
                    for m in range(2):
                        key0 = HEAD * (2 * r + n)
                        done = nc.tensor.transpose(aux[:, 1, S * n + P * m:S * n + P * m + P],
                                                   vpad[:, m, key0:key0 + P], ident)
                done.then_inc(v_turned, 1)

            def q_stat(g):
                b = 1 + g
                pe.wait_ge(acc_read[b % 2], b // 2 + 1)
                if g:
                    pe.wait_ge(p_copied, 4 * g)
                else:
                    pe.wait_ge(v_copied, 2)
                for t in range(4):
                    for n in range(NWIN):
                        for half in range(2):
                            done = nc.tensor.matmul(QSTAT[HEAD * half:HEAD * half + HEAD, NWIN * t + n:NWIN * t + n + 1],
                                                    qsq[:, t, HEAD * n:HEAD * n + HEAD],
                                                    head_ones[:, HEAD * half:HEAD * half + 1], start=True, stop=True,
                                                    skip_group_check=True)
                done.then_inc(q_summed, 1)

            def scores(j):
                g, t = divmod(j, 4)
                pe.wait_ge(kdup_loaded, 64)
                if j:
                    pe.wait_ge(biased, j)
                for n in range(NWIN):
                    k0 = HEAD if n == 0 else 0
                    done = nc.tensor.matmul(aux[:, 0, P * n + k0:P * n + P], qbd[:, t, n, :],
                                            kdup[:, g, HEAD * (n - 1) + k0:HEAD * (n + 1)], start=True, stop=True,
                                            skip_group_check=True)
                done.then_inc(scored, 1)

            def turn_p(j):
                pe.wait_ge(probs_made, j + 1)
                if j:
                    pe.wait_ge(p_copied, j)
                for n in range(NWIN):
                    done = nc.tensor.transpose(aux[:, 1, P * n:P * n + P], pr[j % 2][:, n, :], ident)
                done.then_inc(p_turned, 1)

            def values(j):
                g = j // 4
                pe.wait_ge(p_copied, j + 1)
                if j:
                    pe.wait_ge(a_made, j)
                for n in range(NWIN):
                    for half in range(2):
                        col = S * (j % 2) + HEAD * n
                        done = nc.tensor.matmul(aux[HEAD * half:HEAD * half + HEAD, 2, col:col + HEAD],
                                                vtok[:, n, HEAD * g:HEAD * g + HEAD],
                                                pt[j % 2][:, n, HEAD * half:HEAD * half + HEAD], start=True, stop=True,
                                                skip_group_check=True)
                done.then_inc(o_summed, 1)

            def attn_after(u):
                b, s = divmod(u, 8)
                if b == 1 and s == 1:
                    pe.wait_ge(acc_read[0], 1)
                    nc.tensor.matmul(aux[:, 0, :], head_ones, ksq.rearrange("p m s -> p (m s)"), start=True,
                                     stop=True).then_inc(k_summed, 1)
                if b == 1 and s in (2, 3):
                    turn_v(s - 2)
                if 2 <= b < 2 + KV_HEADS:
                    g, j = b - 2, 4 * (b - 2)
                    if s == 1:
                        q_stat(g)
                        scores(j)
                    if s == 2:
                        scores(j + 1)
                    if s == 3:
                        turn_p(j)
                        scores(j + 2)
                    if s == 4:
                        values(j)
                        turn_p(j + 1)
                        scores(j + 3)
                    if s == 5:
                        values(j + 1)
                        turn_p(j + 2)
                        values(j + 2)
                        turn_p(j + 3)
                        values(j + 3)

            def run(st, activations, after_unit, i=0, looped=False):
                sums = st.sums_after() if not looped else {}
                for u in range(st.units):
                    b, v = divmod(u, st.block_units)
                    block = st.block0 + b
                    if v == 0:
                        wait_sums_free(block, i)
                    hi, lo, wait_group = activations(b)
                    if v % 2 == 0 and wait_group is not None:
                        wait_group(v // 2)
                    unit(st, u, hi, lo, KU * v, v == 0, v == st.block_units - 1, block % 2, i)
                    if u in sums:
                        ada_sum(st.ada0 // KC + sums[u], False)
                    if looped and st.ada_items and u == BODY_SUM_AFTER:
                        ada_sum(st.ada0 // KC, True, i)
                    after_unit(u)

            def use_h(sub, first):
                wait = (lambda kg: pe.wait_ge(h_made, 4 * sub + kg + 1)) if first else None
                return h_hi, h_lo, wait

            def use_a(count, per_group, first):
                wait = (lambda kg: pe.wait_ge(a_made, count + per_group * (kg + 1))) if first else None
                return a_hi, a_lo, wait

            run(ATTN, lambda b: use_h(0, b == 0) if b < QKV_BLOCKS else use_a(0, 4, b == QKV_BLOCKS), attn_after)

            def ffn(layer):
                sub, a0 = 2 * layer + 1, A_COUNT[layer]
                norm_stat(sub)
                for ph, (up, down) in enumerate(FFN[layer]):
                    run(up, lambda b: use_h(sub, ph == 0 and b == 0), lambda u: None, looped=True)
                    with pe.Fori(1, up.repeat) as i:
                        run(up, lambda b: use_h(sub, False), lambda u: None, i, looped=True)

                    def after_down(u):
                        if layer == 1 and ph == 2 and u in OUT_TURNS:
                            turn_out(OUT_TURNS.index(u))
                    run(down, lambda b: use_a(a0, 1, b == 0), after_down)
                    a0 += up.repeat

            def turn_out(b):
                block = FFN1[2][1].block0 + b
                pe.wait_ge(acc_read[block % 2], block // 2 + 1)
                if b:
                    pe.wait_ge(out_copied, b)
                for n in range(2):
                    for t in range(4):
                        done = nc.tensor.transpose(aux[:, n, P * t:P * t + P], x[:, 4 * b + t, P * n:P * n + P], ident)
                done.then_inc(out_turned, 1)

            ffn(0)

            def sgu_after(u):
                if u == 32:
                    pe.wait_ge(parts_made, 16)
                    for n in range(2):
                        for b in range(4):
                            done = nc.tensor.matmul(VSTAT[:, n:n + 1], parts[:, b, P * n:P * n + P], ones[:, 0:1],
                                                    start=b == 0, stop=b == 3, skip_group_check=True)
                    done.then_inc(vstat_summed, 1)
                if 33 <= u < 41 and u % 2 == 1:
                    k = (u - 33) // 2
                    pe.wait_ge(ws_loaded[k % 2], 32 * (k // 2 + 1))
                    if k:
                        pe.wait_ge(ws_masked, k)
                    else:
                        pe.wait_ge(vroot_made, 1)
                    for t in range(4):
                        done = nc.tensor.transpose(aux[:, 2, P * t:P * t + P], ws_raw[k % 2][:, t, :], ident)
                    done.then_inc(ws_turned, 1)
                    if k:
                        pe.wait_ge(sv_made, k)
                    for n in range(2):
                        for t in range(4):
                            done = nc.tensor.transpose(aux[:, n, P * t:P * t + P],
                                                       vbuf[:, 4 * k + t, P * n:P * n + P], ident)
                    done.then_inc(vt_turned, 1)
                if 33 <= u < 41 and u % 2 == 0:
                    k = (u - 34) // 2
                    pe.wait_ge(vt_copied, k + 1)
                    pe.wait_ge(ws_masked, k + 1)
                    for t in range(4):
                        for n in range(2):
                            done = nc.tensor.matmul(MIXED[:, t, P * n:P * n + P], v_tokens(k)[:, n, P * t:P * t + P],
                                                    ws_t[:, t, :], start=True, stop=True, skip_group_check=True)
                    done.then_inc(mixed, 1)

            norm_stat(2)
            run(SGU, lambda b: use_h(2, b == 0) if b < 2 * OUT_BLOCKS else use_a(A_SGU, 1, b == 2 * OUT_BLOCKS),
                sgu_after)
            ffn(1)
            for b in range(OUT_BLOCKS):
                if OUT_TURNS[b] >= FFN1[2][1].units:
                    turn_out(b)


def constant_tiles():
    i = np.arange(P)
    half = i // HEAD
    tiles = np.zeros((P, 5, P), np.float32)
    tiles[:, 0] = np.eye(P)
    tiles[:, 1] = 1
    tiles[:, 2] = half[:, None] == half[None, :]
    tiles[:, 3] = np.abs(i[:, None] % HEAD + HEAD - i[None, :])
    tiles[:, 4] = half[None, :] >= half[:, None]
    return tiles


def constant_slopes():
    slope = -(2.0 ** (-8.0 * np.arange(1, HEADS + 1) / HEADS)).astype(np.float32)
    return np.ascontiguousarray(np.repeat(slope.reshape(PAIRS, 2).T, HEAD, axis=0))


INPUTS = ["x", "c", "w_ada", "b_ada", "attn_w_qkv", "attn_q_gain", "attn_k_gain", "attn_sinks", "attn_w_o",
          "sgu_w_in", "sgu_v_gain", "sgu_w_s", "sgu_b_s", "sgu_w_out", "ffn_w_gate", "ffn_w_up", "ffn_w_down"]


def kernel(**inputs):
    import concourse.bacc as bacc
    from concourse.bass_utils import run_bass_kernel_spmd

    nc = bacc.Bacc("TRN2", target_bir_lowering=False, num_devices=1)
    arrays = {f"in_{name}": np.ascontiguousarray(inputs[name]) for name in INPUTS}
    arrays["const_tiles"] = constant_tiles()
    arrays["const_slopes"] = constant_slopes()
    args = [nc.dram_tensor(name, a.shape, F32, kind="ExternalInput").ap() for name, a in arrays.items()]
    result = nc.dram_tensor("out", (1, S, D), F32, kind="ExternalOutput").ap()
    trunk(nc, *args, result)
    r = run_bass_kernel_spmd(nc, [arrays], core_ids=[0])
    return r.results[0]["out"]
```

```python
from contextlib import ExitStack

import numpy as np

import concourse.bass as bass
from concourse import mybir
from concourse.alu_op_type import AluOpType as ALU

F32 = mybir.dt.float32
F32R = mybir.dt.float32r
ACT = mybir.ActivationFunctionType
AX = mybir.AxisListType

P = 128
D = 2048
S = 256
DT = D // P
FF = 5632
HEAD = 64
HEADS = D // HEAD
KV_HEADS = 4
PAIRS = HEADS // 2
NWIN = S // HEAD
GROUPS = 16
EPS = 1e-6
NMOD = 6
SH1, SC1, G1, SH2, SC2, G2 = range(NMOD)

RING = 8
KC = 2
NB = 512
BT = NB // P
SPLIT = 4
KI = DT // KC
AHEAD = 4
ADA_BLOCKS = NMOD * D // NB
ADA_PER_VECTOR = D // NB
MOD_COLS = NMOD * D // P
PHASES = [4, 4, 3]

QKV_BLOCKS = (HEADS + 2 * KV_HEADS) * HEAD // NB
OUT_BLOCKS = D // NB

def scores_after(j):
    group, t = divmod(j, PAIRS // KV_HEADS)
    return 8 * (group + 2) + 1 + 2 * t


SCORES_AT = {scores_after(j): j for j in range(PAIRS)}
OUT_AT = {scores_after(j) + 1: j for j in range(PAIRS)}
TURN_AT = {scores_after(j) + 3: j for j in range(PAIRS)}
VALUES_AT = {scores_after(j) + 4: j for j in range(PAIRS)}
OUT_ORDER = [(0, 0), (0, 1), (0, 2), (1, 0), (1, 1), (1, 2), (0, 3), (1, 3)]
OUT_DONE = {53: 0, 55: 1, 63: 2, 71: 3}
ATTN_UNITS = ([(b, k) for b in range(QKV_BLOCKS) for k in range(KI)] +
              [(QKV_BLOCKS + b, 2 * k + n) for b, k in OUT_ORDER for n in range(2)] +
              [(QKV_BLOCKS + b, k) for b in (2, 3) for k in range(KI)])

PRO_ITEMS = 2 * ADA_PER_VECTOR * KI


def weave(units, steps):
    done = [min(steps, steps * (u + 1) // (units - 2)) for u in range(units)]
    return [b - a for a, b in zip([0] + done, done)]


ATTN_RATES = [(21, 3.3), (56, 1.7), (70, 4.2), (72, 0)]


def weave_rates(rates, steps):
    per_unit = []
    for end, rate in rates:
        per_unit += [rate] * (end - len(per_unit))
    total, done, out = sum(per_unit), 0.0, []
    for r in per_unit:
        out.append(int((done + r) * steps / total + 1e-6) - int(done * steps / total + 1e-6))
        done += r
    return out


ATTN_STEPS = weave_rates(ATTN_RATES, 3 * ADA_PER_VECTOR * DT)
BODY_STEPS = [0, 0, 1, 1, 2, 1, 1, 2, 1, 1, 2, 1, 1, 2, 0, 0]
BODY_SUM_AFTER = 11


def ring_order(steps):
    order, taken = [], 0
    for u, n in enumerate(steps):
        order.append(("w", u))
        for _ in range(n):
            if taken % KC == 0:
                order.append(("a", taken // KC))
            taken += 1
    return order


class Stretch:

    def __init__(self, before, units, steps, block_units, repeat=1):
        self.units, self.steps, self.repeat, self.block_units = units, steps, repeat, block_units
        self.order = ring_order(steps)
        self.per_body = len(self.order)
        self.ada_items = sum(steps) // KC
        self.item0, self.unit0, self.block0, self.ada0 = before
        self.end = (self.item0 + self.per_body * repeat, self.unit0 + units * repeat,
                    self.block0 + units // block_units * repeat, self.ada0 + self.ada_items * repeat)

    def place(self, r, i=0):
        return (self.item0 + r) % RING, (self.item0 + r) // RING + 1 + (self.per_body // RING) * i

    def places(self, kind, i=0):
        return {n: self.place(r, i) for r, (k, n) in enumerate(self.order) if k == kind}

    def sums_after(self):
        done, found = 0, {}
        for u, n in enumerate(self.steps):
            for _ in range(n):
                done += 1
                if done % DT == 0:
                    found[max(u - 2, 0)] = done // DT - 1
        return found


def plan():
    attn = Stretch((PRO_ITEMS, 0, 0, PRO_ITEMS), 72, ATTN_STEPS, 8)
    at = attn.end
    ffns = []
    for layer in range(2):
        if layer:
            sgu = Stretch(at, 96, weave(96, 128), 8)
            at = sgu.end
        phases = []
        for ph, blocks in enumerate(PHASES):
            woven = layer == 0 or ph == 0
            up = Stretch(at, 16, BODY_STEPS if woven else [0] * 16, 8, blocks)
            n = 8 * blocks
            down = Stretch(up.end, n, weave(n, ([32, 32, 16] if layer == 0 else [0] * 3)[ph]), 2 * blocks)
            at = down.end
            phases.append((up, down))
        ffns.append(phases)
    return attn, ffns[0], sgu, ffns[1]


ATTN, FFN0, SGU, FFN1 = plan()
FFN = [FFN0, FFN1]
A_COUNT = [PAIRS, PAIRS + sum(PHASES) + 4]
A_SGU = PAIRS + sum(PHASES)
OUT_TURNS = [FFN1[2][1].block_units * (b + 1) + 2 for b in range(4)]
NORM_BLOCKS = [0, 4, 8, 16]


def trunk(nc, x_in, c_in, w_ada, b_ada, w_qkv, q_gain, k_gain, sinks, w_o, w_in, v_gain, w_s, b_s, w_out,
          w_gate, w_up, w_down, const_tiles, const_slopes, out):
    ctx = ExitStack()
    with ctx:
        def sb(name, shape, dt=F32):
            return ctx.enter_context(nc.sbuf_tensor(name, shape, dt))

        def sem(name):
            return ctx.enter_context(nc.semaphore(name))

        x = sb("x", [P, DT, S])
        h_hi = sb("h_hi", [P, DT, S], F32R)
        h_lo = sb("h_lo", [P, DT, S], F32R)
        a_hi = sb("a_hi", [P, DT, S], F32R)
        a_lo = sb("a_lo", [P, DT, S], F32R)
        ring = [sb(f"ring{s}", [P, KC, NB]) for s in range(RING)]
        w_hi = [sb(f"w_hi{s}", [P, KC, NB], F32R) for s in range(SPLIT)]
        w_lo = [sb(f"w_lo{s}", [P, KC, NB], F32R) for s in range(SPLIT)]
        ada = sb("ada", [P, 2, 2, NB])
        consts = sb("consts", [P, 5, P])
        ident, ones, head_ones, dist, mask = (consts[:, i, :] for i in range(5))
        slopes = sb("slopes", [P, PAIRS])
        sinkt = sb("sinkt", [P, PAIRS])
        mod = sb("mod", [P, 2 * MOD_COLS])
        bias_t = sb("bias_t", [P, 2 * MOD_COLS])
        c_act = sb("c_act", [P, DT])
        vgain = sb("vgain", [P, DT])
        gains = sb("gains", [P, 2])
        kgain = sb("kgain", [P, 1])
        epst = sb("epst", [P, 1])
        root = sb("root", [P, S])
        rstd = sb("rstd", [P, S])
        small = sb("small", [P, 80])
        qrstd, qroot, smax, den, inv = (small[:, a:b] for a, b in ((0, 16), (16, 32), (32, 36), (36, 40), (40, 44)))
        negmax, expsum, sinkexp = ([small[:, a + 4 * i:a + 4 * i + 4] for i in range(2)] for a in (44, 52, 60))
        vroot, vrstd = small[:, 68:70], small[:, 70:72]
        sink_row = sb("sink_row", [1, HEADS])
        work = sb("work", [P, 10752])

        def area(start, *shape):
            n = int(np.prod(shape))
            v = work[:, start:start + n]
            if len(shape) == 2:
                v = v.rearrange("p (a b) -> p a b", a=shape[0])
            if len(shape) == 3:
                v = v.rearrange("p (a b c) -> p a b c", a=shape[0], b=shape[1])
            return v

        x_tok = area(0, 2, D)
        rows = area(4096, 4, P)
        sq = area(4608, BT, S)
        parts = area(5632, BT, S)
        xr = [area(6656, BT, S), area(7680, BT, S)]
        hf = [area(8704, BT, S), area(9728, BT, S)]
        gate, hid = xr
        x_out = [area(0, 2, NB), area(1024, 2, NB)]
        qbd = area(0, PAIRS // KV_HEADS, NWIN, P)
        kdup = area(2048, KV_HEADS, S)
        vtok = area(3072, NWIN, S)
        pt = [area(4096 + 512 * i, NWIN, P) for i in range(2)]
        sc = [area(5120 + 512 * i, NWIN, P) for i in range(2)]
        pr = [area(6144 + 512 * i, NWIN, P) for i in range(2)]
        qsq = area(7168, BT, S)
        vpad = area(8192, 2, S + HEAD)
        kraw = area(8832, 2, S)
        ksq = area(9344, 2, S)
        abias = [area(9856 + P * i, P) for i in range(2)]
        krstd = area(10112, 512)
        vbuf = area(0, DT, S)
        bs_b = [area(4096, 4, P), area(10240, 4, P)]
        ugate, yf = xr
        ws_raw = [area(8704, 4, P), area(9216, 4, P)]
        ws_t = area(9728, 4, P)

        acc = ctx.enter_context(nc.psum_tensor("acc", [P, 2, BT, S], F32))
        aux = ctx.enter_context(nc.psum_tensor("aux", [P, 4, 512], F32))
        ADA_COLS = aux[:, 3, 0:2 * MOD_COLS]
        TURNED = aux[:, 1, 0:256]
        MIXED = aux[:, 0:2, :].rearrange("p b (t s) -> p (b t) s", t=2)
        VSTAT = aux[:, 2, 0:2]
        QSTAT = aux[:, 1, 0:16]

        consts_loaded = sem("consts_loaded")
        rows_loaded = sem("rows_loaded")
        x_loaded = sem("x_loaded")
        loaded = [sem(f"loaded{s}") for s in range(RING)]
        kdup_loaded = sem("kdup_loaded")
        ws_loaded = [sem("ws_loaded0"), sem("ws_loaded1")]
        out_stored = [sem("out_stored0"), sem("out_stored1")]
        hi_made = sem("hi_made")
        lo_made = sem("lo_made")
        units_done = sem("units_done")
        ada_steps = sem("ada_steps")
        ada_summed = sem("ada_summed")
        mod_made = sem("mod_made")
        acc_read = [sem("acc_read0"), sem("acc_read1")]
        eps_made = sem("eps_made")
        c_made = sem("c_made")
        vecs_loaded = sem("vecs_loaded")
        vecs_copied = sem("vecs_copied")
        bias_made = sem("bias_made")
        rows_turned = sem("rows_turned")
        kgain_made = sem("kgain_made")
        x_turned = sem("x_turned")
        x_copied = sem("x_copied")
        out_turned = sem("out_turned")
        out_copied = sem("out_copied")
        squared = sem("squared")
        parts_made = sem("parts_made")
        stat_summed = sem("stat_summed")
        root_made = sem("root_made")
        rstd_made = sem("rstd_made")
        xr_made = sem("xr_made")
        hf_made = sem("hf_made")
        h_hi_made = sem("h_hi_made")
        h_made = sem("h_made")
        att_cleared = sem("att_cleared")
        k_summed = sem("k_summed")
        k_root = sem("k_root")
        k_recip = sem("k_recip")
        k_normed = sem("k_normed")
        v_turned = sem("v_turned")
        v_copied = sem("v_copied")
        q_summed = sem("q_summed")
        q_root = sem("q_root")
        q_recip = sem("q_recip")
        abias_made = sem("abias_made")
        scored = sem("scored")
        biased = sem("biased")
        max_made = sem("max_made")
        negmax_made = sem("negmax_made")
        exp_made = sem("exp_made")
        den_made = sem("den_made")
        inv_made = sem("inv_made")
        probs_made = sem("probs_made")
        p_turned = sem("p_turned")
        p_copied = sem("p_copied")
        o_summed = sem("o_summed")
        y_made = sem("y_made")
        a_hi_made = sem("a_hi_made")
        a_made = sem("a_made")
        vstat_summed = sem("vstat_summed")
        vroot_made = sem("vroot_made")
        vrstd_made = sem("vrstd_made")
        ws_turned = sem("ws_turned")
        ws_masked = sem("ws_masked")
        vt_turned = sem("vt_turned")
        vt_copied = sem("vt_copied")
        mixed = sem("mixed")
        sv_made = sem("sv_made")

        block = ctx.enter_context(nc.Block())

        def mod_col(layer, m, tile):
            return layer * MOD_COLS + m * DT + tile

        def vector_made(layer, m):
            return (layer * NMOD + m + 1) * ADA_PER_VECTOR

        def rows_over(ap, n):
            return ap.unsqueeze(1).to_broadcast([P, n, ap.shape[1]])

        def v_tokens(k):
            return area(BT * S * k, 2, NB)


        @block.sync
        def _(sp):
            def groups_of(w):
                return w.rearrange("(g k p) n -> g p k n", k=KC, p=P)

            qkv_v, wo_v, win_v, wout_v = (groups_of(w[0]) for w in (w_qkv, w_o, w_in, w_out))
            gate_v, up_v, down_v = ([groups_of(w[l]) for l in range(2)] for w in (w_gate, w_up, w_down))
            ada_v = [groups_of(w_ada[l]) for l in range(2)]

            def columns(v, b):
                return v[:, :, bass.ds(NB * b, NB)]

            held = [None] * RING

            def send(slot, source, kind, number):
                if held[slot] is not None and held[slot][0] == "w":
                    sp.wait_ge(lo_made, held[slot][1] + 1)
                elif held[slot] is not None:
                    sp.wait_ge(ada_steps, KC * held[slot][1] + KC)
                sp.dma_start(ring[slot][:], source).then_inc(loaded[slot], 16)
                held[slot] = (kind, number)

            def send_body(st, unit_source, i=0):
                q0 = st.ada0 // KI
                for r, (kind, n) in enumerate(st.order):
                    slot = st.place(r)[0]
                    if kind == "w":
                        send(slot, unit_source(n, i), "w", st.unit0 + st.units * i + n)
                    else:
                        layer, b = divmod(q0 + n // KI, ADA_BLOCKS)
                        send(slot, columns(ada_v[layer][n % KI], b + i), "a", st.ada0 + st.ada_items * i + n)

            sp.wait_ge(rows_loaded, 16)
            for n in range(PRO_ITEMS):
                send(n % RING, columns(ada_v[0][n % KI], n // KI), "a", n)

            def attn_unit(n, i):
                b, k = ATTN_UNITS[n]
                if b == 0:
                    return columns(qkv_v[k], QKV_BLOCKS - 1)
                return columns(qkv_v[k], b - 1) if b < QKV_BLOCKS else columns(wo_v[k], b - QKV_BLOCKS)

            def sgu_unit(n, i):
                b, k = divmod(n, KI)
                if b < 2 * OUT_BLOCKS:
                    return columns(win_v[k], (b + OUT_BLOCKS) % (2 * OUT_BLOCKS))
                return columns(wout_v[k], b - 2 * OUT_BLOCKS)

            def send_ffn(layer):
                for ph, (up, down) in enumerate(FFN[layer]):
                    def up_unit(n, i):
                        return columns((gate_v, up_v)[n // KI][layer][n % KI], PHASES[0] * ph + i)

                    def down_unit(n, i):
                        b, k = divmod(n, down.block_units)
                        return columns(down_v[layer][BT // KC * PHASES[0] * ph + k], b)

                    send_body(up, up_unit)
                    first = list(held)
                    body_of = {"w": up.units, "a": up.ada_items}
                    with sp.Fori(1, up.repeat) as i:
                        held[:] = [(kind, n + body_of[kind] * (i - 1)) for kind, n in first]
                        send_body(up, up_unit, i)
                    held[:] = [(kind, n + body_of[kind] * (up.repeat - 1)) for kind, n in first]
                    send_body(down, down_unit)

            send_body(ATTN, attn_unit)
            send_ffn(0)
            send_body(SGU, sgu_unit)
            send_ffn(1)

            out_v = out[0].rearrange("(b p) n -> p b n", p=P)
            for b in range(OUT_BLOCKS):
                sp.wait_ge(out_copied, b + 1)
                sp.dma_start(out_v[:, :, NB * b:NB * (b + 1)], x_out[b % 2]).then_inc(out_stored[b % 2], 16)
            for s in range(2):
                sp.wait_ge(out_stored[s], 16 * (OUT_BLOCKS // 2))

        @block.gpsimd
        def _(pool):
            nc.gpsimd.memset(epst[:], EPS).then_inc(eps_made, 1)
            pool.wait_ge(h_made, 4)
            nc.gpsimd.memset(qbd, 0.0)
            nc.gpsimd.memset(vpad[:, :, 0:HEAD], 0.0)
            for i in range(2):
                nc.gpsimd.memset(sc[i][:, 0, 0:HEAD], -1e30)
                last = nc.gpsimd.memset(pr[i][:, 0, 0:HEAD], 0.0)
            last.then_inc(att_cleared, 1)
            ws_v = w_s[0].rearrange("(k g) t s -> k t g s", g=4)
            bs_v = b_s[0].rearrange("(k g) t -> k (g t)", g=4)
            pool.wait_ge(h_made, 12)
            for k in range(4):
                if k >= 2:
                    pool.wait_ge(ws_turned, k - 1)
                    pool.wait_ge(sv_made, k - 1)
                pool.dma_start(ws_raw[k % 2], ws_v[k]).then_inc(ws_loaded[k % 2], 16)
                pool.dma_start(bs_b[k % 2].rearrange("p g t -> p (g t)"), bs_v[k].partition_broadcast(P))\
                    .then_inc(ws_loaded[k % 2], 16)

        @block.scalar
        def _(act):
            act.dma_start(rows[0:DT, 0, :], c_in.rearrange("b (t p) -> (b t) p", p=P)).then_inc(rows_loaded, 16)
            act.dma_start(consts[:], const_tiles).then_inc(consts_loaded, 16)
            act.dma_start(x_tok, x_in[0].rearrange("(b p) n -> p b n", p=P)).then_inc(x_loaded, 16)
            act.dma_start(rows[0:DT, 1, :], v_gain.rearrange("b (t p) -> (b t) p", p=P)).then_inc(vecs_loaded, 16)
            for l in range(2):
                act.dma_start(rows[0:MOD_COLS, 2 + l, :], b_ada[l].rearrange("(t p) -> t p", p=P))\
                    .then_inc(vecs_loaded, 16)
            act.dma_start(slopes[:], const_slopes).then_inc(vecs_loaded, 16)
            act.dma_start(sink_row[:], sinks).then_inc(vecs_loaded, 16)
            for half in range(2):
                for i, g in enumerate((q_gain, k_gain)):
                    act.dma_start(gains[HEAD * half:HEAD * half + HEAD, i:i + 1], g.rearrange("a d -> d a"))\
                        .then_inc(vecs_loaded, 16)

            act.wait_ge(rows_turned, 1)
            nc.scalar.activation(c_act[:], TURNED[:, 0:DT], ACT.Silu).then_inc(c_made, 1)

            def square_block(n, source):
                if n:
                    act.wait_ge(parts_made, n)
                nc.scalar.activation(sq, source, ACT.Square).then_inc(squared, 1)

            def square_x(sub, b):
                square_block(NORM_BLOCKS[sub] + b, x[:, 4 * b:4 * b + 4, :])

            for b in range(4):
                act.wait_ge(x_turned, b + 1)
                nc.scalar.copy(x[:, 4 * b:4 * b + 4, :], acc[:, b % 2]).then_inc(x_copied, 1)

            act.wait_ge(rows_turned, 2)
            nc.scalar.copy(vgain[:], TURNED[:, DT:2 * DT])
            nc.scalar.copy(bias_t[:], TURNED[:, 2 * DT:2 * DT + 2 * MOD_COLS])
            nc.scalar.copy(sinkt[:], TURNED[:, 240:240 + PAIRS]).then_inc(vecs_copied, 1)

            for b in range(4):
                act.wait_ge(x_copied, b + 1)
                square_x(0, b)

            def norm_root(sub):
                act.wait_ge(stat_summed, sub + 1)
                act.wait_ge(eps_made, 1)
                nc.scalar.activation(root[:], aux[:, 2, 0:S], ACT.Sqrt, bias=epst[:], scale=1.0 / D)\
                    .then_inc(root_made, 1)

            def modulate(sub, g):
                layer, n = sub // 2, 4 * sub + g
                scale, shift = (mod_col(layer, m, 4 * g) for m in ((SC1, SC2)[sub % 2], (SH1, SH2)[sub % 2]))
                act.wait_ge(xr_made, n + 1)
                act.wait_ge(mod_made, vector_made(layer, (SC1, SC2)[sub % 2]))
                if g >= 2:
                    act.wait_ge(h_made, n - 1)
                for t in range(BT):
                    last = nc.scalar.activation(hf[g % 2][:, t, :], xr[g % 2][:, t, :], ACT.Identity,
                                                bias=mod[:, shift + t:shift + t + 1],
                                                scale=mod[:, scale + t:scale + t + 1])
                last.then_inc(hf_made, 1)
                act.wait_ge(hf_made, n + 1)
                nc.scalar.copy(h_hi[:, 4 * g:4 * g + 4, :], hf[g % 2]).then_inc(h_hi_made, 1)

            def start_norm(sub):
                norm_root(sub)
                modulate(sub, 0)
                modulate(sub, 1)

            def split_hi(st, u, i=0):
                slot, round_ = st.places("w", i)[u]
                unit = st.unit0 + st.units * i + u
                act.wait_ge(loaded[slot], 16 * round_)
                if st.unit0 + u >= SPLIT:
                    act.wait_ge(units_done, unit + 1 - SPLIT)
                nc.scalar.copy(w_hi[u % SPLIT][:], ring[slot][:]).then_inc(hi_made, 1)

            def split_stretch(st, after_last, after_unit, i=0):
                for u in range(st.units):
                    if u == AHEAD - 1:
                        after_last()
                    if u >= AHEAD:
                        after_unit(u - AHEAD)
                    split_hi(st, u, i)

            def with_norm(sub, after_unit):
                def after(u):
                    if u in (0, 2):
                        modulate(sub, 2 + u // 2)
                    after_unit(u)
                return after

            def read_kv():
                act.wait_ge(units_done, 8)
                act.wait_ge(att_cleared, 1)
                nc.scalar.copy(kraw, acc[:, 0, 0:2, :])
                nc.scalar.activation(ksq, acc[:, 0, 0:2, :], ACT.Square)
                nc.scalar.copy(vpad[:, :, HEAD:], acc[:, 0, 2:4, :]).then_inc(acc_read[0], 1)

            def read_q(g):
                b = 1 + g
                act.wait_ge(units_done, 8 * (b + 1))
                act.wait_ge(att_cleared, 1)
                if g:
                    act.wait_ge(scored, 4 * g)
                for half in range(2):
                    hp = slice(HEAD * half, HEAD * half + HEAD)
                    nc.scalar.copy(qbd[hp, :, :, HEAD * half:HEAD * half + HEAD].rearrange("p t n q -> p (t n) q"),
                                   acc[hp, b % 2].rearrange("p t (n q) -> p (t n) q", q=HEAD))
                nc.scalar.activation(qsq, acc[:, b % 2], ACT.Square).then_inc(acc_read[b % 2], 1)

            def bias_of(j):
                if j >= 2:
                    act.wait_ge(biased, j - 1)
                nc.scalar.activation(abias[j % 2], dist, ACT.Copy, scale=slopes[:, j:j + 1]).then_inc(abias_made, 1)

            def exps(j):
                act.wait_ge(negmax_made, j + 1)
                if j >= 2:
                    act.wait_ge(p_turned, j - 1)
                for n in range(NWIN):
                    k0 = HEAD if n == 0 else 0
                    nc.scalar.activation(pr[j % 2][:, n, k0:], sc[j % 2][:, n, k0:], ACT.Exp,
                                         bias=negmax[j % 2][:, n:n + 1], accum_out=expsum[j % 2][:, n:n + 1])
                nc.scalar.activation(sinkexp[j % 2], negmax[j % 2], ACT.Exp, bias=sinkt[:, j:j + 1])\
                    .then_inc(exp_made, 1)

            def copy_turned(j):
                act.wait_ge(p_turned, j + 1)
                if j >= 2:
                    act.wait_ge(o_summed, j - 1)
                nc.scalar.copy(pt[j % 2], aux[:, 1, :].rearrange("p (n q) -> p n q", n=NWIN)).then_inc(p_copied, 1)

            def o_hi(j):
                act.wait_ge(o_summed, j + 1)
                nc.scalar.copy(a_hi[:, j, :], aux[:, 2, S * (j % 2):S * (j % 2) + S]).then_inc(a_hi_made, 1)

            def after_out(b, block, sub):
                act.wait_ge(acc_read[block % 2], block // 2 + 1)
                square_x(sub, b)

            def attn_after(u):
                b, s = divmod(u, 8)
                if u == 7:
                    read_kv()
                elif s == 7 and b < QKV_BLOCKS:
                    read_q(b - 1)
                if u in OUT_DONE:
                    after_out(OUT_DONE[u], QKV_BLOCKS + OUT_DONE[u], 1)
                if b == 1 and s == 1:
                    act.wait_ge(k_summed, 1)
                    nc.scalar.activation(krstd, aux[:, 0, :], ACT.Sqrt, bias=epst[:], scale=1.0 / HEAD)\
                        .then_inc(k_root, 1)
                if b == 1 and s in (2, 3):
                    act.wait_ge(v_turned, s - 1)
                    nc.scalar.copy(vtok[:, 2 * (s - 2):2 * (s - 2) + 2, :],
                                   aux[:, 1, :].rearrange("p (n d) -> p n d", n=2)).then_inc(v_copied, 1)
                if u == 10:
                    act.wait_ge(k_normed, 1)
                    kd = kdup.rearrange("p (m two) s -> p two m s", two=2)
                    for half in range(2):
                        for to in range(2):
                            act.dma_start(kd[HEAD * to:HEAD * to + HEAD, half], kraw[HEAD * half:HEAD * half + HEAD])\
                                .then_inc(kdup_loaded, 16)
                if u in TURN_AT:
                    copy_turned(TURN_AT[u])
                if u in VALUES_AT:
                    o_hi(VALUES_AT[u])
                if u in SCORES_AT:
                    j = SCORES_AT[u]
                    if j % 4 == 0:
                        act.wait_ge(q_summed, j // 4 + 1)
                        nc.scalar.activation(qroot, QSTAT, ACT.Sqrt, bias=epst[:], scale=1.0 / HEAD)\
                            .then_inc(q_root, 1)
                    if j == 0:
                        bias_of(0)
                    exps(j)
                    if j + 1 < PAIRS:
                        bias_of(j + 1)

            split_stretch(ATTN, lambda: start_norm(0), with_norm(0, attn_after))

            def ffn(layer, start):
                sub, a0 = 2 * layer + 1, A_COUNT[layer]
                after_last = start
                for ph, (up, down) in enumerate(FFN[layer]):
                    gp, upp = up.block0 % 2, (up.block0 + 1) % 2

                    def after_up(i):
                        act.wait_ge(acc_read[upp], (up.block0 + 1) // 2 + 1 + i)
                        nc.scalar.copy(a_hi[:, bass.ds(4 * i, 4), :], hid).then_inc(a_hi_made, 1)

                    def after_gate(i):
                        act.wait_ge(units_done, up.unit0 + up.units * i + 8)
                        act.wait_ge(acc_read[upp], (up.block0 + 1) // 2 + i)
                        nc.scalar.activation(gate, acc[:, gp], ACT.Silu).then_inc(acc_read[gp], 1)

                    def body(i, after_last, norm):
                        def after_unit(u):
                            if u == 7:
                                after_gate(i)
                        split_stretch(up, after_last, with_norm(sub, after_unit) if norm else after_unit, i)

                    body(0, after_last, ph == 0)
                    with act.Fori(1, up.repeat) as i:
                        body(i, lambda: after_up(i - 1), False)

                    def after_down(u):
                        b, s = divmod(u, down.block_units)
                        if ph == 2 and s == down.block_units - 1 and layer == 0:
                            after_out(b, down.block0 + b, 2)
                        if ph == 2 and layer == 1 and u in OUT_TURNS:
                            store_block(OUT_TURNS.index(u))

                    split_stretch(down, lambda: after_up(up.repeat - 1), after_down)
                    after_last = lambda: None

            def store_block(b):
                act.wait_ge(out_turned, b + 1)
                if b >= 2:
                    act.wait_ge(out_stored[b % 2], 16)
                nc.scalar.copy(x_out[b % 2], aux[:, 0:2, :]).then_inc(out_copied, 1)

            def next_norm(sub, last_block):
                def f():
                    after_out(3, last_block, sub)
                    start_norm(sub)
                return f

            ffn(0, next_norm(1, ATTN.end[2] - 1))

            def sgu_after(u):
                b, s = divmod(u, 8)
                block = SGU.block0 + b
                par = block % 2
                if s == 7 and b < 4:
                    act.wait_ge(units_done, SGU.unit0 + u + 1)
                    nc.scalar.activation(vbuf[:, 4 * b:4 * b + 4, :], acc[:, par], ACT.Gelu).then_inc(acc_read[par], 1)
                    act.wait_ge(acc_read[par], block // 2 + 1)
                    square_block(12 + b, vbuf[:, 4 * b:4 * b + 4, :])
                elif s == 7 and b < 8:
                    act.wait_ge(units_done, SGU.unit0 + u + 1)
                    if b > 4:
                        act.wait_ge(y_made, b - 4)
                    nc.scalar.activation(ugate, acc[:, par], ACT.Gelu).then_inc(acc_read[par], 1)
                    act.wait_ge(y_made, b - 3)
                    nc.scalar.copy(a_hi[:, 4 * (b - 4):4 * (b - 4) + 4, :], yf).then_inc(a_hi_made, 1)
                elif s == 7:
                    after_out(b - 8, block, 3)
                if u == 32:
                    act.wait_ge(vstat_summed, 1)
                    nc.scalar.activation(vroot, VSTAT, ACT.Sqrt, bias=epst[:], scale=1.0 / D).then_inc(vroot_made, 1)
                if 33 <= u < 41 and u % 2 == 1:
                    k = (u - 33) // 2
                    act.wait_ge(vrstd_made, 1)
                    act.wait_ge(vt_turned, k + 1)
                    for n in range(2):
                        last = nc.scalar.activation(v_tokens(k)[:, n, :], aux[:, n, :], ACT.Copy,
                                                    scale=vrstd[:, n:n + 1])
                    last.then_inc(vt_copied, 1)

            split_stretch(SGU, next_norm(2, FFN0[2][1].end[2] - 1), with_norm(2, sgu_after))
            ffn(1, next_norm(3, SGU.end[2] - 1))
            for b in range(OUT_BLOCKS):
                if OUT_TURNS[b] >= FFN1[2][1].units - AHEAD:
                    store_block(b)

        @block.vector
        def _(dve):
            def reduce_block(n, read_by, times):
                dve.wait_ge(squared, n + 1)
                if times:
                    dve.wait_ge(read_by, times)
                nc.vector.tensor_reduce(out=parts[:, n % 4, :], in_=sq.rearrange("p t s -> p s t"), axis=AX.X,
                                        op=ALU.add).then_inc(parts_made, 1)

            def reduce_x(sub, b):
                reduce_block(NORM_BLOCKS[sub] + b, *((vstat_summed, 1) if sub == 3 else (stat_summed, sub)))

            def ada_step(q, s, slot, round_, looped, after_loop, i=0):
                parts_n = 1 if looped else 2
                buf = 0 if looped else q % 2
                into = ada[:, buf, s % parts_n, :]
                if s % KC == 0:
                    dve.wait_ge(loaded[slot], 16 * round_)
                weight, scale = ring[slot][:, s % KC, :], c_act[:, s:s + 1]
                if s < parts_n:
                    if looped or after_loop or q >= 2:
                        dve.wait_ge(ada_summed, q + i - (0 if looped or after_loop else 1))
                    nc.vector.tensor_scalar(into, weight, scale, None, ALU.mult).then_inc(ada_steps, 1)
                else:
                    dve.wait_ge(ada_steps, DT * (q + i) + s - parts_n + 1)
                    nc.vector.scalar_tensor_tensor(out=into, in0=weight, scalar=scale, in1=into,
                                                   op0=ALU.mult, op1=ALU.add).then_inc(ada_steps, 1)

            def make_mod(q, i=0):
                cols = bass.ds(BT * q + BT * i, BT)
                dve.wait_ge(ada_summed, q + i + 1)
                nc.vector.tensor_tensor(mod[:, cols], ADA_COLS[:, cols], bias_t[:, cols], ALU.add)\
                    .then_inc(mod_made, 1)

            def update_x(layer, m, b, block, end_unit):
                g = mod_col(layer, m, 4 * b)
                dve.wait_ge(units_done, end_unit)
                dve.wait_ge(mod_made, vector_made(layer, m))
                for t in range(BT):
                    xt = x[:, 4 * b + t, :]
                    last = nc.vector.scalar_tensor_tensor(out=xt, in0=acc[:, block % 2, t, :],
                                                          scalar=mod[:, g + t:g + t + 1], in1=xt,
                                                          op0=ALU.mult, op1=ALU.add)
                last.then_inc(acc_read[block % 2], 1)

            def norm_x(sub, g):
                if g == 0:
                    dve.wait_ge(root_made, sub + 1)
                    nc.vector.reciprocal(rstd[:], root[:]).then_inc(rstd_made, 1)
                    dve.wait_ge(rstd_made, sub + 1)
                if g >= 2:
                    dve.wait_ge(h_hi_made, 4 * sub + g - 1)
                nc.vector.tensor_tensor(xr[g % 2], x[:, 4 * g:4 * g + 4, :], rows_over(rstd[:], BT), ALU.mult)\
                    .then_inc(xr_made, 1)

            def h_lo_of(sub, g):
                n = 4 * sub + g
                dve.wait_ge(h_hi_made, n + 1)
                nc.vector.tensor_tensor(h_lo[:, 4 * g:4 * g + 4, :], hf[g % 2],
                                        h_hi[:, 4 * g:4 * g + 4, :].bitcast(F32), ALU.subtract).then_inc(h_made, 1)

            def start_norm(sub):
                norm_x(sub, 0)
                norm_x(sub, 1)
                h_lo_of(sub, 0)
                norm_x(sub, 2)
                h_lo_of(sub, 1)

            def with_norm(sub, after_unit):
                def after(u):
                    if u == 0:
                        norm_x(sub, 3)
                        h_lo_of(sub, 2)
                    if u == 2:
                        h_lo_of(sub, 3)
                    after_unit(u)
                return after

            def split_lo(st, u, i=0):
                slot = st.places("w")[u][0]
                dve.wait_ge(hi_made, st.unit0 + st.units * i + u + 1)
                nc.vector.tensor_tensor(w_lo[u % SPLIT][:], ring[slot][:], w_hi[u % SPLIT][:].bitcast(F32),
                                        ALU.subtract).then_inc(lo_made, 1)

            def split_stretch(st, after_last, after_unit, i=0, looped=False, after_loop=False):
                step, sums = 0, st.sums_after()
                if looped:
                    sums = {BODY_SUM_AFTER: 0} if st.ada_items else {}
                for u in range(st.units):
                    if u == AHEAD - 1:
                        after_last()
                    if u >= AHEAD:
                        after_unit(u - AHEAD)
                    if u - AHEAD in sums:
                        make_mod(st.ada0 // KI + sums[u - AHEAD], i)
                    split_lo(st, u, i)
                    for _ in range(st.steps[u]):
                        q, s = divmod(step, DT)
                        ada_step(st.ada0 // KI + q, s, *st.places("a", i)[step // KC], looped,
                                 after_loop and q == 0, i)
                        step += 1

            for q in range(PRO_ITEMS // KI):
                for s in range(DT):
                    if q == 0 and s == 0:
                        dve.wait_ge(c_made, 1)
                    n = KI * q + s // KC
                    ada_step(q, s, n % RING, n // RING + 1, False, False)
                if q == 1:
                    dve.wait_ge(vecs_copied, 1)
                    scale_bias = bias_t[:].rearrange("p (l h m t) -> p (l h) m t", l=2, h=2, t=DT)[:, :, SC1, :]
                    nc.vector.tensor_scalar(scale_bias, scale_bias, 1.0, None, ALU.add).then_inc(bias_made, 1)
                    dve.wait_ge(bias_made, 1)
                if q:
                    make_mod(q - 1)
                if 3 <= q < 7:
                    reduce_x(0, q - 3)
            make_mod(PRO_ITEMS // KI - 1)

            def norm_k():
                dve.wait_ge(vecs_loaded, 16 * 9)
                nc.vector.scalar_tensor_tensor(out=kgain[:], in0=gains[:, 0:1], scalar=HEAD ** -0.5,
                                               in1=gains[:, 1:2], op0=ALU.mult, op1=ALU.mult).then_inc(kgain_made, 1)
                dve.wait_ge(k_root, 1)
                nc.vector.reciprocal(krstd, krstd).then_inc(k_recip, 1)
                dve.wait_ge(k_recip, 1)
                dve.wait_ge(kgain_made, 1)
                kf = kraw.rearrange("p m s -> p (m s)")
                nc.vector.scalar_tensor_tensor(out=kf, in0=kf, scalar=kgain[:], in1=krstd,
                                               op0=ALU.mult, op1=ALU.mult).then_inc(k_normed, 1)

            def softmax_in(j):
                t, n_pairs = j % 4, PAIRS // KV_HEADS
                dve.wait_ge(scored, j + 1)
                dve.wait_ge(abias_made, j + 1)
                if j >= 2:
                    dve.wait_ge(exp_made, j - 1)
                for n in range(NWIN):
                    k0 = HEAD if n == 0 else 0
                    last = nc.vector.scalar_tensor_tensor(
                        out=sc[j % 2][:, n, k0:], in0=aux[:, 0, P * n + k0:P * n + P],
                        scalar=qrstd[:, n_pairs * t + n:n_pairs * t + n + 1], in1=abias[j % 2][:, k0:],
                        op0=ALU.mult, op1=ALU.add)
                last.then_inc(biased, 1)
                dve.wait_ge(biased, j + 1)
                nc.vector.tensor_reduce(out=smax, in_=sc[j % 2], axis=AX.X, op=ALU.max).then_inc(max_made, 1)
                dve.wait_ge(max_made, j + 1)
                nc.vector.tensor_scalar(negmax[j % 2], smax, sinkt[:, j:j + 1], -1.0, ALU.max, ALU.mult)\
                    .then_inc(negmax_made, 1)

            def softmax_out(j):
                dve.wait_ge(exp_made, j + 1)
                nc.vector.tensor_tensor(den, expsum[j % 2], sinkexp[j % 2], ALU.add).then_inc(den_made, 1)
                dve.wait_ge(den_made, j + 1)
                nc.vector.reciprocal(inv, den).then_inc(inv_made, 1)
                dve.wait_ge(inv_made, j + 1)
                nc.vector.tensor_tensor(pr[j % 2], pr[j % 2], inv.unsqueeze(2).to_broadcast([P, NWIN, P]), ALU.mult)\
                    .then_inc(probs_made, 1)

            def o_lo(j):
                dve.wait_ge(a_hi_made, j + 1)
                nc.vector.tensor_tensor(a_lo[:, j, :], aux[:, 2, S * (j % 2):S * (j % 2) + S],
                                        a_hi[:, j, :].bitcast(F32), ALU.subtract).then_inc(a_made, 1)

            def after_out(layer, m, b, block, end_unit, sub):
                update_x(layer, m, b, block, end_unit)
                reduce_x(sub, b)

            def attn_after(u):
                b, s = divmod(u, 8)
                if u in OUT_DONE:
                    after_out(0, G1, OUT_DONE[u], QKV_BLOCKS + OUT_DONE[u], u + 1, 1)
                if b == 1 and s == 1:
                    norm_k()
                if u in OUT_AT:
                    softmax_out(OUT_AT[u])
                if u in SCORES_AT:
                    j = SCORES_AT[u]
                    if j % 4 == 0:
                        dve.wait_ge(q_root, j // 4 + 1)
                        nc.vector.reciprocal(qrstd, qroot).then_inc(q_recip, 1)
                        dve.wait_ge(q_recip, j // 4 + 1)
                    softmax_in(j)
                if u in VALUES_AT:
                    o_lo(VALUES_AT[u])

            split_stretch(ATTN, lambda: start_norm(0), with_norm(0, attn_after))

            def ffn(layer, start):
                sub, a0 = 2 * layer + 1, A_COUNT[layer]
                after_last = start
                done = 0
                for ph, (up, down) in enumerate(FFN[layer]):
                    gp, upp = up.block0 % 2, (up.block0 + 1) % 2

                    def multiply_up(i):
                        dve.wait_ge(units_done, up.unit0 + up.units * (i + 1))
                        dve.wait_ge(acc_read[gp], up.block0 // 2 + 1 + i)
                        nc.vector.tensor_tensor(hid, acc[:, upp], gate, ALU.mult).then_inc(acc_read[upp], 1)

                    def hidden_lo(i):
                        dve.wait_ge(a_hi_made, a0 + done + i + 1)
                        nc.vector.tensor_tensor(a_lo[:, bass.ds(4 * i, 4), :], hid,
                                                a_hi[:, bass.ds(4 * i, 4), :].bitcast(F32), ALU.subtract)\
                            .then_inc(a_made, 1)

                    def body(i, after_last, norm, previous=None):
                        def after_unit(u):
                            if u == 0 and previous is not None:
                                hidden_lo(previous)
                        split_stretch(up, after_last, with_norm(sub, after_unit) if norm else after_unit, i,
                                      looped=True)

                    body(0, after_last, ph == 0)
                    with dve.Fori(1, up.repeat) as i:
                        body(i, lambda: multiply_up(i - 1), False, i - 1)

                    def after_block(b, down=down, ph=ph):
                        end = down.unit0 + down.block_units * (b + 1)
                        if ph == 2 and layer == 0:
                            after_out(layer, G2, b, down.block0 + b, end, 2)
                        else:
                            update_x(layer, G2, b, down.block0 + b, end)

                    def after_down(u):
                        if u == 0:
                            hidden_lo(up.repeat - 1)
                        if (u + 1) % down.block_units == 0:
                            after_block(u // down.block_units)

                    split_stretch(down, lambda: multiply_up(up.repeat - 1), after_down, after_loop=True)
                    done += up.repeat
                    after_last = lambda after_block=after_block: after_block(3)
                    yield_last = after_last
                return yield_last

            def next_norm(sub, last):
                def f():
                    last()
                    start_norm(sub)
                return f

            last = ffn(0, next_norm(1, lambda: after_out(
                0, G1, 3, ATTN.end[2] - 1, ATTN.units, 1)))

            def sgu_after(u):
                b, s = divmod(u, 8)
                block = SGU.block0 + b
                if s == 7 and b < 4:
                    reduce_block(12 + b, stat_summed, 3)
                elif s == 7 and b < 8:
                    dve.wait_ge(acc_read[block % 2], block // 2 + 1)
                    dve.wait_ge(sv_made, b - 3)
                    nc.vector.tensor_tensor(yf, ugate, vbuf[:, 4 * (b - 4):4 * (b - 4) + 4, :], ALU.mult)\
                        .then_inc(y_made, 1)
                    dve.wait_ge(a_hi_made, A_SGU + b - 3)
                    nc.vector.tensor_tensor(a_lo[:, 4 * (b - 4):4 * (b - 4) + 4, :], yf,
                                            a_hi[:, 4 * (b - 4):4 * (b - 4) + 4, :].bitcast(F32), ALU.subtract)\
                        .then_inc(a_made, 1)
                elif s == 7:
                    after_out(1, G1, b - 8, block, SGU.unit0 + u + 1, 3)
                if u == 32:
                    dve.wait_ge(vroot_made, 1)
                    nc.vector.reciprocal(vrstd, vroot).then_inc(vrstd_made, 1)
                if 33 <= u < 41 and u % 2 == 1:
                    k = (u - 33) // 2
                    dve.wait_ge(ws_turned, k + 1)
                    if k:
                        dve.wait_ge(mixed, k)
                    nc.vector.tensor_tensor(ws_t, aux[:, 2, :].rearrange("p (g t) -> p g t", g=4),
                                            rows_over(mask, 4), ALU.mult).then_inc(ws_masked, 1)
                if 33 <= u < 41 and u % 2 == 0:
                    k = (u - 34) // 2
                    dve.wait_ge(mixed, k + 1)
                    dve.wait_ge(ws_loaded[k % 2], 32 * (k // 2 + 1))
                    for t in range(4):
                        last = nc.vector.scalar_tensor_tensor(
                            out=vbuf[:, 4 * k + t, :].rearrange("p (n t) -> p n t", n=2),
                            in0=MIXED[:, t, :].rearrange("p (n t) -> p n t", n=2),
                            scalar=vgain[:, 4 * k + t:4 * k + t + 1], in1=rows_over(bs_b[k % 2][:, t, :], 2),
                            op0=ALU.mult, op1=ALU.add)
                    last.then_inc(sv_made, 1)

            split_stretch(SGU, next_norm(2, last),
                          with_norm(2, sgu_after), after_loop=True)
            last = ffn(1, next_norm(3, lambda: after_out(
                1, G1, 3, SGU.end[2] - 1, SGU.end[1], 3)))
            last()

        @block.tensor
        def _(pe):
            def unit(st, u, act_hi, act_lo, kt, first, last_, par, i=0):
                pe.wait_ge(lo_made, st.unit0 + st.units * i + u + 1)
                hi, lo = w_hi[u % SPLIT], w_lo[u % SPLIT]
                for k in range(KC):
                    for t in range(BT):
                        cols, sums = slice(P * t, P * t + P), acc[:, par, t, :]
                        start = first and k == 0 and t % 2 == 0
                        stop = last_ and k == KC - 1
                        nc.tensor.matmul(sums, hi[:, k, cols], act_hi[:, kt + k, :], start=start, stop=False,
                                         skip_group_check=True)
                        nc.tensor.matmul(sums, hi[:, k, cols], act_lo[:, kt + k, :], start=False, stop=False,
                                         skip_group_check=True)
                        done = nc.tensor.matmul(sums, lo[:, k, cols], act_hi[:, kt + k, :], start=False, stop=stop,
                                                skip_group_check=True)
                done.then_inc(units_done, 1)

            def wait_sums_free(block, i=0):
                if block < 2:
                    pe.wait_ge(x_copied, 4)
                else:
                    pe.wait_ge(acc_read[block % 2], block // 2 + i)

            def ada_sum(q, looped, i=0):
                parts_n, buf = (1, 0) if looped else (2, q % 2)
                pe.wait_ge(ada_steps, DT * (q + i + 1))
                if looped or q:
                    pe.wait_ge(mod_made, q + i)
                for t in range(BT):
                    for part in range(parts_n):
                        done = nc.tensor.matmul(ADA_COLS[:, bass.ds(BT * q + BT * i + t, 1)],
                                                ada[:, buf, part, P * t:P * t + P], ones[:, 0:1],
                                                start=part == 0, stop=part == parts_n - 1, skip_group_check=True)
                done.then_inc(ada_summed, 1)

            def norm_stat(sub):
                pe.wait_ge(parts_made, NORM_BLOCKS[sub] + 4)
                for b in range(4):
                    done = nc.tensor.matmul(aux[:, 2, 0:S], ones, parts[:, b, :], start=b == 0, stop=b == 3)
                done.then_inc(stat_summed, 1)

            pe.wait_ge(consts_loaded, 16)
            pe.wait_ge(rows_loaded, 16)
            nc.tensor.transpose(TURNED[:, 0:DT], rows[0:DT, 0, :], ident[0:DT, 0:DT]).then_inc(rows_turned, 1)
            pe.wait_ge(x_loaded, 16)
            for b in range(4):
                if b >= 2:
                    pe.wait_ge(x_copied, b - 1)
                for n in range(2):
                    for t in range(4):
                        done = nc.tensor.transpose(acc[:, b % 2, t, P * n:P * n + P],
                                                   x_tok[:, n, P * (4 * b + t):P * (4 * b + t) + P], ident)
                done.then_inc(x_turned, 1)
            pe.wait_ge(vecs_loaded, 16 * 9)
            pe.wait_ge(c_made, 1)
            nc.tensor.transpose(TURNED[:, DT:2 * DT], rows[0:DT, 1, :], ident[0:DT, 0:DT])
            for l in range(2):
                nc.tensor.transpose(TURNED[:, 2 * DT + MOD_COLS * l:2 * DT + MOD_COLS * (l + 1)],
                                    rows[0:MOD_COLS, 2 + l, :], ident[0:MOD_COLS, 0:MOD_COLS])
            for half in range(2):
                done = nc.tensor.matmul(TURNED[HEAD * half:HEAD * half + HEAD, 240:240 + PAIRS], ones[0:1, 0:HEAD],
                                        sink_row[0:1, half:HEADS:2], start=True, stop=True)
            done.then_inc(rows_turned, 1)
            for q in range(PRO_ITEMS // KI):
                if q == PRO_ITEMS // KI - 1:
                    norm_stat(0)
                ada_sum(q, False)

            def turn_v(r):
                if r:
                    pe.wait_ge(v_copied, r)
                for n in range(2):
                    for m in range(2):
                        key0 = HEAD * (2 * r + n)
                        done = nc.tensor.transpose(aux[:, 1, S * n + P * m:S * n + P * m + P],
                                                   vpad[:, m, key0:key0 + P], ident)
                done.then_inc(v_turned, 1)

            def q_stat(g):
                b = 1 + g
                pe.wait_ge(acc_read[b % 2], b // 2 + 1)
                if g:
                    pe.wait_ge(p_copied, 4 * g - 1)
                else:
                    pe.wait_ge(v_copied, 2)
                for t in range(4):
                    for n in range(NWIN):
                        for half in range(2):
                            done = nc.tensor.matmul(QSTAT[HEAD * half:HEAD * half + HEAD, NWIN * t + n:NWIN * t + n + 1],
                                                    qsq[:, t, HEAD * n:HEAD * n + HEAD],
                                                    head_ones[:, HEAD * half:HEAD * half + 1], start=True, stop=True,
                                                    skip_group_check=True)
                done.then_inc(q_summed, 1)

            def scores(j):
                g, t = divmod(j, 4)
                pe.wait_ge(kdup_loaded, 64)
                if j:
                    pe.wait_ge(biased, j)
                for n in range(NWIN):
                    k0 = HEAD if n == 0 else 0
                    done = nc.tensor.matmul(aux[:, 0, P * n + k0:P * n + P], qbd[:, t, n, :],
                                            kdup[:, g, HEAD * (n - 1) + k0:HEAD * (n + 1)], start=True, stop=True,
                                            skip_group_check=True)
                done.then_inc(scored, 1)

            def turn_p(j):
                pe.wait_ge(probs_made, j + 1)
                if j:
                    pe.wait_ge(p_copied, j)
                pe.wait_ge(q_root, min((j + 1) // 4 + 1, KV_HEADS))
                for n in range(NWIN):
                    done = nc.tensor.transpose(aux[:, 1, P * n:P * n + P], pr[j % 2][:, n, :], ident)
                done.then_inc(p_turned, 1)

            def values(j):
                g = j // 4
                pe.wait_ge(p_copied, j + 1)
                if j:
                    pe.wait_ge(a_made, j)
                for n in range(NWIN):
                    for half in range(2):
                        col = S * (j % 2) + HEAD * n
                        done = nc.tensor.matmul(aux[HEAD * half:HEAD * half + HEAD, 2, col:col + HEAD],
                                                vtok[:, n, HEAD * g:HEAD * g + HEAD],
                                                pt[j % 2][:, n, HEAD * half:HEAD * half + HEAD], start=True, stop=True,
                                                skip_group_check=True)
                done.then_inc(o_summed, 1)

            def attn_after(u):
                b, s = divmod(u, 8)
                if b == 1 and s == 1:
                    pe.wait_ge(acc_read[0], 1)
                    nc.tensor.matmul(aux[:, 0, :], head_ones, ksq.rearrange("p m s -> p (m s)"), start=True,
                                     stop=True).then_inc(k_summed, 1)
                if b == 1 and s in (2, 3):
                    turn_v(s - 2)
                if u in VALUES_AT:
                    values(VALUES_AT[u])
                if u in SCORES_AT:
                    if SCORES_AT[u] % 4 == 0:
                        q_stat(SCORES_AT[u] // 4)
                    scores(SCORES_AT[u])
                if u in TURN_AT:
                    turn_p(TURN_AT[u])

            def run(st, activations, after_unit, i=0, looped=False, order=None):
                sums = st.sums_after() if not looped else {}
                for u in range(st.units):
                    b, v = divmod(u, st.block_units)
                    if order:
                        b, v = order[u]
                    block = st.block0 + b
                    if v == 0:
                        wait_sums_free(block, i)
                    hi, lo, wait_group = activations(b)
                    if v % 2 == 0 and wait_group is not None:
                        wait_group(v // 2)
                    unit(st, u, hi, lo, KC * v, v == 0, v == st.block_units - 1, block % 2, i)
                    if u in sums:
                        ada_sum(st.ada0 // KI + sums[u], False)
                    if looped and st.ada_items and u == BODY_SUM_AFTER:
                        ada_sum(st.ada0 // KI, True, i)
                    after_unit(u)

            def use_h(sub, first):
                wait = (lambda kg: pe.wait_ge(h_made, 4 * sub + kg + 1)) if first else None
                return h_hi, h_lo, wait

            def use_a(count, per_group, first):
                wait = (lambda kg: pe.wait_ge(a_made, count + per_group * (kg + 1))) if first else None
                return a_hi, a_lo, wait

            run(ATTN, lambda b: use_h(0, b == 0) if b < QKV_BLOCKS else use_a(0, 4, b == QKV_BLOCKS), attn_after,
                order=ATTN_UNITS)

            def ffn(layer):
                sub, a0 = 2 * layer + 1, A_COUNT[layer]
                norm_stat(sub)
                for ph, (up, down) in enumerate(FFN[layer]):
                    run(up, lambda b: use_h(sub, ph == 0 and b == 0), lambda u: None, looped=True)
                    with pe.Fori(1, up.repeat) as i:
                        run(up, lambda b: use_h(sub, False), lambda u: None, i, looped=True)

                    def after_down(u):
                        if layer == 1 and ph == 2 and u in OUT_TURNS:
                            turn_out(OUT_TURNS.index(u))
                    run(down, lambda b: use_a(a0, 1, b == 0), after_down)
                    a0 += up.repeat

            def turn_out(b):
                block = FFN1[2][1].block0 + b
                pe.wait_ge(acc_read[block % 2], block // 2 + 1)
                if b:
                    pe.wait_ge(out_copied, b)
                for n in range(2):
                    for t in range(4):
                        done = nc.tensor.transpose(aux[:, n, P * t:P * t + P], x[:, 4 * b + t, P * n:P * n + P], ident)
                done.then_inc(out_turned, 1)

            ffn(0)

            def sgu_after(u):
                if u == 32:
                    pe.wait_ge(parts_made, 16)
                    for n in range(2):
                        for b in range(4):
                            done = nc.tensor.matmul(VSTAT[:, n:n + 1], parts[:, b, P * n:P * n + P], ones[:, 0:1],
                                                    start=b == 0, stop=b == 3, skip_group_check=True)
                    done.then_inc(vstat_summed, 1)
                if 33 <= u < 41 and u % 2 == 1:
                    k = (u - 33) // 2
                    pe.wait_ge(ws_loaded[k % 2], 32 * (k // 2 + 1))
                    if k:
                        pe.wait_ge(ws_masked, k)
                    else:
                        pe.wait_ge(vroot_made, 1)
                    for t in range(4):
                        done = nc.tensor.transpose(aux[:, 2, P * t:P * t + P], ws_raw[k % 2][:, t, :], ident)
                    done.then_inc(ws_turned, 1)
                    if k:
                        pe.wait_ge(sv_made, k)
                    for n in range(2):
                        for t in range(4):
                            done = nc.tensor.transpose(aux[:, n, P * t:P * t + P],
                                                       vbuf[:, 4 * k + t, P * n:P * n + P], ident)
                    done.then_inc(vt_turned, 1)
                if 33 <= u < 41 and u % 2 == 0:
                    k = (u - 34) // 2
                    pe.wait_ge(vt_copied, k + 1)
                    pe.wait_ge(ws_masked, k + 1)
                    for t in range(4):
                        for n in range(2):
                            done = nc.tensor.matmul(MIXED[:, t, P * n:P * n + P], v_tokens(k)[:, n, P * t:P * t + P],
                                                    ws_t[:, t, :], start=True, stop=True, skip_group_check=True)
                    done.then_inc(mixed, 1)

            norm_stat(2)
            run(SGU, lambda b: use_h(2, b == 0) if b < 2 * OUT_BLOCKS else use_a(A_SGU, 1, b == 2 * OUT_BLOCKS),
                sgu_after)
            ffn(1)
            for b in range(OUT_BLOCKS):
                if OUT_TURNS[b] >= FFN1[2][1].units:
                    turn_out(b)


def constant_tiles():
    i = np.arange(P)
    half = i // HEAD
    tiles = np.zeros((P, 5, P), np.float32)
    tiles[:, 0] = np.eye(P)
    tiles[:, 1] = 1
    tiles[:, 2] = half[:, None] == half[None, :]
    tiles[:, 3] = np.abs(i[:, None] % HEAD + HEAD - i[None, :])
    tiles[:, 4] = half[None, :] >= half[:, None]
    return tiles


def constant_slopes():
    slope = -(2.0 ** (-8.0 * np.arange(1, HEADS + 1) / HEADS)).astype(np.float32)
    return np.ascontiguousarray(np.repeat(slope.reshape(PAIRS, 2).T, HEAD, axis=0))


INPUTS = ["x", "c", "w_ada", "b_ada", "attn_w_qkv", "attn_q_gain", "attn_k_gain", "attn_sinks", "attn_w_o",
          "sgu_w_in", "sgu_v_gain", "sgu_w_s", "sgu_b_s", "sgu_w_out", "ffn_w_gate", "ffn_w_up", "ffn_w_down"]


def kernel(**inputs):
    import concourse.bacc as bacc
    from concourse.bass_utils import run_bass_kernel_spmd

    nc = bacc.Bacc("TRN2", target_bir_lowering=False, num_devices=1)
    arrays = {f"in_{name}": np.ascontiguousarray(inputs[name]) for name in INPUTS}
    arrays["const_tiles"] = constant_tiles()
    arrays["const_slopes"] = constant_slopes()
    args = [nc.dram_tensor(name, a.shape, F32, kind="ExternalInput").ap() for name, a in arrays.items()]
    result = nc.dram_tensor("out", (1, S, D), F32, kind="ExternalOutput").ap()
    trunk(nc, *args, result)
    r = run_bass_kernel_spmd(nc, [arrays], core_ids=[0])
    return r.results[0]["out"]
```

```python
from contextlib import ExitStack

import numpy as np

import concourse.bass as bass
from concourse import mybir
from concourse.alu_op_type import AluOpType as ALU

F32 = mybir.dt.float32
F32R = mybir.dt.float32r
ACT = mybir.ActivationFunctionType
AX = mybir.AxisListType

P = 128
D = 2048
S = 256
DT = D // P
HEAD = 64
HEADS = D // HEAD
KV_HEADS = 4
PAIRS = HEADS // 2
NWIN = S // HEAD
EPS = 1e-6
NMOD = 6
SH1, SC1, G1, SH2, SC2, G2 = range(NMOD)

RING = 8
KC = 2
NB = 512
BT = NB // P
SPLIT = 4
KI = DT // KC
AHEAD = 4
ADA_BLOCKS = NMOD * D // NB
ADA_PER_VECTOR = D // NB
MOD_COLS = NMOD * D // P
PHASES = [4, 4, 3]

QKV_BLOCKS = (HEADS + 2 * KV_HEADS) * HEAD // NB
OUT_BLOCKS = D // NB

def scores_after(j):
    group, t = divmod(j, PAIRS // KV_HEADS)
    return 8 * (group + 2) + 1 + 2 * t


def stage(lag, late=(), over_stat=0):
    units = [scores_after(j) + lag + over_stat * (j in (1, 5, 9)) for j in range(PAIRS)]
    units[PAIRS - len(late):] = late
    return {u: j for j, u in enumerate(units)}


STAT_AT = {scores_after(4 * g) - 1: g for g in range(KV_HEADS)}
STAT_TURN_AT = {scores_after(4 * g): g for g in range(KV_HEADS)}
SCORES_AT = stage(0)
SOFTMAX_IN_AT = stage(1, [47])
EXP_AT = stage(2, [48])
SOFTMAX_OUT_AT = stage(3, [49])
TURN_AT = stage(4, [50])
COPY_AT = stage(5, [49, 50])
VALUES_AT = stage(6, [50, 51], 1)
OUT_ORDER = [(0, 0), (0, 1), (1, 0), (1, 1), (0, 2), (1, 2), (0, 3), (1, 3)]
OUT_DONE = {53: 0, 55: 1, 63: 2, 71: 3}
ATTN_UNITS = ([(b, k) for b in range(QKV_BLOCKS) for k in range(KI)] +
              [(QKV_BLOCKS + b, 2 * k + n) for b, k in OUT_ORDER for n in range(2)] +
              [(QKV_BLOCKS + b, k) for b in (2, 3) for k in range(KI)])

V_TURN_AT = {33 + 7 * k: k for k in range(4)}
MIX_AT = {35 + 7 * k: k for k in range(4)}

PARTED_BLOCKS = 5 * ADA_PER_VECTOR
PRO_ITEMS = 2 * ADA_PER_VECTOR * KI


def weave(units, steps, free=2):
    done = [min(steps, steps * (u + 1) // (units - free)) for u in range(units)]
    return [b - a for a, b in zip([0] + done, done)]


ATTN_RATES = [(4, 2), (21, 3.0), (56, 2.7), (66, 3.4), (72, 0)]


def weave_rates(rates, steps):
    per_unit = []
    for end, rate in rates:
        per_unit += [rate] * (end - len(per_unit))
    total, done, out = sum(per_unit), 0.0, []
    for r in per_unit:
        out.append(int((done + r) * steps / total + 1e-6) - int(done * steps / total + 1e-6))
        done += r
    return out


ATTN_STEPS = weave_rates(ATTN_RATES, 3 * ADA_PER_VECTOR * DT)
BODY_STEPS = [0, 0, 1, 1, 2, 1, 1, 2, 1, 1, 2, 1, 1, 2, 0, 0]
BODY_SUM_AFTER = 11


def ada_parts(q):
    return 2 if q < PARTED_BLOCKS else 1


def ring_order(steps):
    order, taken = [], 0
    for u, n in enumerate(steps):
        order.append(("w", u))
        for _ in range(n):
            if taken % KC == 0:
                order.append(("a", taken // KC))
            taken += 1
    return order


class Stretch:

    def __init__(self, before, units, steps, block_units, repeat=1):
        self.units, self.steps, self.repeat, self.block_units = units, steps, repeat, block_units
        self.order = ring_order(steps)
        self.per_body = len(self.order)
        self.ada_items = sum(steps) // KC
        self.item0, self.unit0, self.block0, self.ada0 = before
        self.end = (self.item0 + self.per_body * repeat, self.unit0 + units * repeat,
                    self.block0 + units // block_units * repeat, self.ada0 + self.ada_items * repeat)

    def place(self, r, i=0):
        return (self.item0 + r) % RING, (self.item0 + r) // RING + 1 + (self.per_body // RING) * i

    def places(self, kind, i=0):
        return {n: self.place(r, i) for r, (k, n) in enumerate(self.order) if k == kind}

    def sums_after(self):
        done, found = 0, {}
        for u, n in enumerate(self.steps):
            for _ in range(n):
                done += 1
                if done % DT == 0:
                    found[min(u + 1, self.units - AHEAD - 1)] = done // DT - 1
        return found


def plan():
    attn = Stretch((PRO_ITEMS, 0, 0, PRO_ITEMS), 72, ATTN_STEPS, 8)
    at = attn.end
    ffns = []
    for layer in range(2):
        if layer:
            sgu = Stretch(at, 96, weave(96, 128), 8)
            at = sgu.end
        phases = []
        for ph, blocks in enumerate(PHASES):
            woven = layer == 0 or ph == 0
            up = Stretch(at, 16, BODY_STEPS if woven else [0] * 16, 8, blocks)
            n = 8 * blocks
            down = Stretch(up.end, n, weave(n, ([32, 32, 16] if layer == 0 else [0] * 3)[ph], (2, 2, 8)[ph]), 2 * blocks)
            at = down.end
            phases.append((up, down))
        ffns.append(phases)
    return attn, ffns[0], sgu, ffns[1]


ATTN, FFN0, SGU, FFN1 = plan()
FFN = [FFN0, FFN1]
A_COUNT = [PAIRS, PAIRS + sum(PHASES) + 4]
A_SGU = PAIRS + sum(PHASES)
OUT_TURNS = [FFN1[2][1].block_units * (b + 1) + 2 for b in range(4)]
NORM_BLOCKS = [0, 4, 7, 14]
V_BLOCKS = 10
HT = 2
HP = DT // HT


def trunk(nc, x_in, c_in, w_ada, b_ada, w_qkv, q_gain, k_gain, sinks, w_o, w_in, v_gain, w_s, b_s, w_out,
          w_gate, w_up, w_down, const_tiles, const_slopes, out):
    ctx = ExitStack()
    with ctx:
        def sb(name, shape, dt=F32):
            return ctx.enter_context(nc.sbuf_tensor(name, shape, dt))

        def sem(name):
            return ctx.enter_context(nc.semaphore(name))

        x = sb("x", [P, DT, S])
        h_hi = sb("h_hi", [P, DT, S], F32R)
        h_lo = sb("h_lo", [P, DT, S], F32R)
        a_hi = sb("a_hi", [P, DT, S], F32R)
        a_lo = sb("a_lo", [P, DT, S], F32R)
        ring = [sb(f"ring{s}", [P, KC, NB]) for s in range(RING)]
        w_hi = [sb(f"w_hi{s}", [P, KC, NB], F32R) for s in range(SPLIT)]
        w_lo = [sb(f"w_lo{s}", [P, KC, NB], F32R) for s in range(SPLIT)]
        ada = sb("ada", [P, 2, 2, NB])
        consts = sb("consts", [P, 6, P])
        ident, ones, head_ones, dist, mask, picks = (consts[:, i, :] for i in range(6))
        slopes = sb("slopes", [P, PAIRS])
        sinkt = sb("sinkt", [P, PAIRS])
        mod = sb("mod", [P, 2 * MOD_COLS])
        bias_t = sb("bias_t", [P, 2 * MOD_COLS])
        c_act = sb("c_act", [P, DT])
        vgain = sb("vgain", [P, DT])
        gains = sb("gains", [P, 2])
        kgain = sb("kgain", [P, 1])
        epst = sb("epst", [P, 1])
        root = sb("root", [P, S])
        rstd = sb("rstd", [P, S])
        small = sb("small", [P, 80])
        qrstd, smax, den, inv = (small[:, a:b] for a, b in ((0, 16), (32, 36), (36, 40), (40, 44)))
        negmax, expsum, sinkexp = ([small[:, a + 4 * i:a + 4 * i + 4] for i in range(2)] for a in (44, 52, 60))
        vroot, vrstd = small[:, 68:70], small[:, 70:72]
        sink_row = sb("sink_row", [1, HEADS])
        qroot = sb("qroot", [2 * BT, S])
        work = sb("work", [P, 10752])

        def area(start, *shape):
            n = int(np.prod(shape))
            v = work[:, start:start + n]
            if len(shape) == 2:
                v = v.rearrange("p (a b) -> p a b", a=shape[0])
            if len(shape) == 3:
                v = v.rearrange("p (a b c) -> p a b c", a=shape[0], b=shape[1])
            return v

        x_tok = area(0, 2, D)
        rows = area(4096, 4, P)
        sq = area(4608, BT, S)
        parts = area(5632, BT, S)
        xr = [area(6656, BT, S), area(7680, BT, S)]
        xr_piece = [area(6656 + HT * S * i, HT, S) for i in range(4)]
        hf_piece = [area(8704 + HT * S * i, HT, S) for i in range(4)]
        gate, hid = xr
        x_out = [area(0, 2, NB), area(1024, 2, NB)]
        qbd = area(0, PAIRS // KV_HEADS, NWIN, P)
        kdup = area(2048, KV_HEADS, S)
        vtok = area(3072, NWIN, S)
        pt = [area(4096 + 512 * i, NWIN, P) for i in range(2)]
        sc = [area(5120 + 512 * i, NWIN, P) for i in range(2)]
        pr = [area(6144 + 512 * i, NWIN, P) for i in range(2)]
        qsq = area(7168, BT, S)
        vpad = area(8192, 2, S + HEAD)
        kraw = area(8832, 2, S)
        ksq = area(9344, 2, S)
        abias = [area(9856 + P * i, P) for i in range(2)]
        krstd = area(10112, 512)
        vbuf = area(0, DT, S)
        bs_b = [area(4096, 4, P), area(10240, 4, P)]
        ugate, yf = xr
        ws_raw = [area(8704, 4, P), area(9216, 4, P)]
        ws_t = area(9728, 4, P)

        acc = ctx.enter_context(nc.psum_tensor("acc", [P, 2, BT, S], F32))
        aux = ctx.enter_context(nc.psum_tensor("aux", [P, 4, 512], F32))
        ADA_COLS = aux[:, 3, 0:2 * MOD_COLS]
        TURNED = aux[:, 1, 0:256]
        MIXED = aux[:, 0:2, :].rearrange("p b (t s) -> p (b t) s", t=2)
        VSTAT = aux[:, 2, 0:2]
        QSTAT = aux[0:2 * BT, 2, 0:S]
        QTURNED = aux[:, 2, S:S + NWIN * 2 * BT]

        consts_loaded = sem("consts_loaded")
        rows_loaded = sem("rows_loaded")
        x_loaded = sem("x_loaded")
        loaded = [sem(f"loaded{s}") for s in range(RING)]
        kdup_loaded = sem("kdup_loaded")
        ws_loaded = [sem("ws_loaded0"), sem("ws_loaded1")]
        out_stored = [sem("out_stored0"), sem("out_stored1")]
        hi_made = sem("hi_made")
        lo_made = sem("lo_made")
        units_done = sem("units_done")
        ada_steps = sem("ada_steps")
        ada_summed = sem("ada_summed")
        mod_made = sem("mod_made")
        acc_read = [sem("acc_read0"), sem("acc_read1")]
        eps_made = sem("eps_made")
        c_made = sem("c_made")
        vecs_loaded = sem("vecs_loaded")
        vecs_copied = sem("vecs_copied")
        bias_made = sem("bias_made")
        rows_turned = sem("rows_turned")
        kgain_made = sem("kgain_made")
        x_turned = sem("x_turned")
        x_copied = sem("x_copied")
        out_turned = sem("out_turned")
        out_copied = sem("out_copied")
        squared = sem("squared")
        x_updated = sem("x_updated")
        tile_squared = sem("tile_squared")
        parts_made = sem("parts_made")
        stat_summed = sem("stat_summed")
        root_made = sem("root_made")
        rstd_made = sem("rstd_made")
        xr_made = sem("xr_made")
        hf_made = sem("hf_made")
        h_hi_made = sem("h_hi_made")
        h_made = sem("h_made")
        att_cleared = sem("att_cleared")
        k_summed = sem("k_summed")
        k_root = sem("k_root")
        k_recip = sem("k_recip")
        k_normed = sem("k_normed")
        v_turned = sem("v_turned")
        v_copied = sem("v_copied")
        q_squared = sem("q_squared")
        q_summed = sem("q_summed")
        q_root = sem("q_root")
        q_turned = sem("q_turned")
        q_recip = sem("q_recip")
        abias_made = sem("abias_made")
        scored = sem("scored")
        biased = sem("biased")
        max_made = sem("max_made")
        negmax_made = sem("negmax_made")
        exp_made = sem("exp_made")
        den_made = sem("den_made")
        inv_made = sem("inv_made")
        probs_made = sem("probs_made")
        p_turned = sem("p_turned")
        p_copied = sem("p_copied")
        o_summed = sem("o_summed")
        y_made = sem("y_made")
        a_hi_made = sem("a_hi_made")
        a_made = sem("a_made")
        vstat_summed = sem("vstat_summed")
        vroot_made = sem("vroot_made")
        vrstd_made = sem("vrstd_made")
        ws_turned = sem("ws_turned")
        ws_masked = sem("ws_masked")
        vt_turned = sem("vt_turned")
        vt_copied = sem("vt_copied")
        mixed = sem("mixed")
        sv_made = sem("sv_made")

        block = ctx.enter_context(nc.Block())

        def mod_col(layer, m, tile):
            return layer * MOD_COLS + m * DT + tile

        def vector_made(layer, m):
            return (layer * NMOD + m + 1) * ADA_PER_VECTOR

        def rows_over(ap, n):
            return ap.unsqueeze(1).to_broadcast([P, n, ap.shape[1]])

        def v_tokens(k):
            return area(BT * S * k, 2, NB)


        @block.sync
        def _(sp):
            def groups_of(w):
                return w.rearrange("(g k p) n -> g p k n", k=KC, p=P)

            qkv_v, wo_v, win_v, wout_v = (groups_of(w[0]) for w in (w_qkv, w_o, w_in, w_out))
            gate_v, up_v, down_v = ([groups_of(w[l]) for l in range(2)] for w in (w_gate, w_up, w_down))
            ada_v = [groups_of(w_ada[l]) for l in range(2)]

            def columns(v, b):
                return v[:, :, bass.ds(NB * b, NB)]

            held = [None] * RING

            def send(slot, source, kind, number):
                if held[slot] is not None and held[slot][0] == "w":
                    sp.wait_ge(lo_made, held[slot][1] + 1)
                elif held[slot] is not None:
                    sp.wait_ge(ada_steps, KC * held[slot][1] + KC)
                sp.dma_start(ring[slot][:], source).then_inc(loaded[slot], 16)
                held[slot] = (kind, number)

            def send_body(st, unit_source, i=0):
                q0 = st.ada0 // KI
                for r, (kind, n) in enumerate(st.order):
                    slot = st.place(r)[0]
                    if kind == "w":
                        send(slot, unit_source(n, i), "w", st.unit0 + st.units * i + n)
                    else:
                        layer, b = divmod(q0 + n // KI, ADA_BLOCKS)
                        send(slot, columns(ada_v[layer][n % KI], b + i), "a", st.ada0 + st.ada_items * i + n)

            sp.wait_ge(rows_loaded, 16)
            for n in range(PRO_ITEMS):
                send(n % RING, columns(ada_v[0][n % KI], n // KI), "a", n)

            def attn_unit(n, i):
                b, k = ATTN_UNITS[n]
                if b == 0:
                    return columns(qkv_v[k], QKV_BLOCKS - 1)
                return columns(qkv_v[k], b - 1) if b < QKV_BLOCKS else columns(wo_v[k], b - QKV_BLOCKS)

            def sgu_unit(n, i):
                b, k = divmod(n, KI)
                if b < 2 * OUT_BLOCKS:
                    return columns(win_v[k], (b + OUT_BLOCKS) % (2 * OUT_BLOCKS))
                return columns(wout_v[k], b - 2 * OUT_BLOCKS)

            def send_ffn(layer):
                for ph, (up, down) in enumerate(FFN[layer]):
                    def up_unit(n, i):
                        return columns((gate_v, up_v)[n // KI][layer][n % KI], PHASES[0] * ph + i)

                    def down_unit(n, i):
                        b, k = divmod(n, down.block_units)
                        return columns(down_v[layer][BT // KC * PHASES[0] * ph + k], b)

                    send_body(up, up_unit)
                    first = list(held)
                    body_of = {"w": up.units, "a": up.ada_items}
                    with sp.Fori(1, up.repeat) as i:
                        held[:] = [(kind, n + body_of[kind] * (i - 1)) for kind, n in first]
                        send_body(up, up_unit, i)
                    held[:] = [(kind, n + body_of[kind] * (up.repeat - 1)) for kind, n in first]
                    send_body(down, down_unit)

            send_body(ATTN, attn_unit)
            send_ffn(0)
            send_body(SGU, sgu_unit)
            send_ffn(1)

            out_v = out[0].rearrange("(b p) n -> p b n", p=P)
            for b in range(OUT_BLOCKS):
                sp.wait_ge(out_copied, b + 1)
                sp.dma_start(out_v[:, :, NB * b:NB * (b + 1)], x_out[b % 2]).then_inc(out_stored[b % 2], 16)
            for s in range(2):
                sp.wait_ge(out_stored[s], 16 * (OUT_BLOCKS // 2))

        @block.gpsimd
        def _(pool):
            nc.gpsimd.memset(epst[:], EPS).then_inc(eps_made, 1)
            pool.wait_ge(h_made, HP)
            nc.gpsimd.memset(qbd, 0.0)
            nc.gpsimd.memset(vpad[:, :, 0:HEAD], 0.0)
            for i in range(2):
                nc.gpsimd.memset(sc[i][:, 0, 0:HEAD], -1e30)
                last = nc.gpsimd.memset(pr[i][:, 0, 0:HEAD], 0.0)
            last.then_inc(att_cleared, 1)
            ws_v = w_s[0].rearrange("(k g) t s -> k t g s", g=4)
            bs_v = b_s[0].rearrange("(k g) t -> k (g t)", g=4)
            pool.wait_ge(h_made, 3 * HP)
            for k in range(4):
                if k >= 2:
                    pool.wait_ge(ws_turned, k - 1)
                    pool.wait_ge(sv_made, k - 1)
                pool.dma_start(ws_raw[k % 2], ws_v[k]).then_inc(ws_loaded[k % 2], 16)
                pool.dma_start(bs_b[k % 2].rearrange("p g t -> p (g t)"), bs_v[k].partition_broadcast(P))\
                    .then_inc(ws_loaded[k % 2], 16)

        @block.scalar
        def _(act):
            act.dma_start(rows[0:DT, 0, :], c_in.rearrange("b (t p) -> (b t) p", p=P)).then_inc(rows_loaded, 16)
            act.dma_start(consts[:], const_tiles).then_inc(consts_loaded, 16)
            act.dma_start(x_tok, x_in[0].rearrange("(b p) n -> p b n", p=P)).then_inc(x_loaded, 16)
            act.dma_start(rows[0:DT, 1, :], v_gain.rearrange("b (t p) -> (b t) p", p=P)).then_inc(vecs_loaded, 16)
            for l in range(2):
                act.dma_start(rows[0:MOD_COLS, 2 + l, :], b_ada[l].rearrange("(t p) -> t p", p=P))\
                    .then_inc(vecs_loaded, 16)
            act.dma_start(slopes[:], const_slopes).then_inc(vecs_loaded, 16)
            act.dma_start(sink_row[:], sinks).then_inc(vecs_loaded, 16)
            for half in range(2):
                for i, g in enumerate((q_gain, k_gain)):
                    act.dma_start(gains[HEAD * half:HEAD * half + HEAD, i:i + 1], g.rearrange("a d -> d a"))\
                        .then_inc(vecs_loaded, 16)

            act.wait_ge(rows_turned, 1)
            nc.scalar.activation(c_act[:], TURNED[:, 0:DT], ACT.Silu).then_inc(c_made, 1)

            def square_block(n, source):
                if n:
                    act.wait_ge(parts_made, n)
                for sub in (1, 2):
                    if n == NORM_BLOCKS[sub] + 3:
                        act.wait_ge(stat_summed, sub + 1)
                nc.scalar.activation(sq, source, ACT.Square).then_inc(squared, 1)

            def square_x(sub, b):
                square_block(NORM_BLOCKS[sub] + b, x[:, 4 * b:4 * b + 4, :])

            for b in range(4):
                act.wait_ge(x_turned, b + 1)
                nc.scalar.copy(x[:, 4 * b:4 * b + 4, :], acc[:, b % 2]).then_inc(x_copied, 1)

            act.wait_ge(rows_turned, 2)
            nc.scalar.copy(vgain[:], TURNED[:, DT:2 * DT])
            nc.scalar.copy(bias_t[:], TURNED[:, 2 * DT:2 * DT + 2 * MOD_COLS])
            nc.scalar.copy(sinkt[:], TURNED[:, 240:240 + PAIRS]).then_inc(vecs_copied, 1)

            for b in range(4):
                act.wait_ge(x_copied, b + 1)
                square_x(0, b)

            def square_tiles(sub, block):
                act.wait_ge(parts_made, NORM_BLOCKS[sub] + 3)
                for t in range(BT):
                    if t < BT - 1:
                        act.wait_ge(x_updated, (BT - 1) * (sub - 1) + t + 1)
                    else:
                        act.wait_ge(acc_read[block % 2], block // 2 + 1)
                    nc.scalar.activation(sq[:, t, :], x[:, DT - BT + t, :], ACT.Square).then_inc(tile_squared, 1)

            def norm_root(sub):
                act.wait_ge(stat_summed, sub + 1)
                act.wait_ge(eps_made, 1)
                nc.scalar.activation(root[:], aux[:, 2, 0:S], ACT.Sqrt, bias=epst[:], scale=1.0 / D)\
                    .then_inc(root_made, 1)

            def modulate(sub, k):
                layer, n = sub // 2, HP * sub + k
                scale, shift = (mod_col(layer, m, HT * k) for m in ((SC1, SC2)[sub % 2], (SH1, SH2)[sub % 2]))
                act.wait_ge(xr_made, n + 1)
                act.wait_ge(mod_made, vector_made(layer, (SC1, SC2)[sub % 2]))
                if k >= 4:
                    act.wait_ge(h_made, n - 3)
                for t in range(HT):
                    last = nc.scalar.activation(hf_piece[k % 4][:, t, :], xr_piece[k % 4][:, t, :], ACT.Identity,
                                                bias=mod[:, shift + t:shift + t + 1],
                                                scale=mod[:, scale + t:scale + t + 1])
                last.then_inc(hf_made, 1)
                act.wait_ge(hf_made, n + 1)
                nc.scalar.copy(h_hi[:, HT * k:HT * k + HT, :], hf_piece[k % 4]).then_inc(h_hi_made, 1)

            def start_norm(sub):
                if sub:
                    norm_root(sub)
                modulate(sub, 0)
                modulate(sub, 1)

            def split_hi(st, u, i=0):
                slot, round_ = st.places("w", i)[u]
                unit = st.unit0 + st.units * i + u
                act.wait_ge(loaded[slot], 16 * round_)
                if st.unit0 + u >= SPLIT:
                    act.wait_ge(units_done, unit + 1 - SPLIT)
                nc.scalar.copy(w_hi[u % SPLIT][:], ring[slot][:]).then_inc(hi_made, 1)

            def split_stretch(st, after_last, after_unit, i=0, norm=None, later=lambda u: None):
                for u in range(st.units):
                    if u == (AHEAD - 1 if st.unit0 else 1):
                        after_last()
                    if u >= AHEAD:
                        after_unit(u - AHEAD)
                    split_hi(st, u, i)
                    if norm is not None and 2 <= u - 1 < HP:
                        modulate(norm, u - 1)
                    if u >= AHEAD:
                        later(u - AHEAD)

            norm_root(0)

            def read_kv():
                act.wait_ge(units_done, 8)
                act.wait_ge(att_cleared, 1)
                nc.scalar.copy(kraw, acc[:, 0, 0:2, :])
                nc.scalar.activation(ksq, acc[:, 0, 0:2, :], ACT.Square)
                nc.scalar.copy(vpad[:, :, HEAD:], acc[:, 0, 2:4, :]).then_inc(acc_read[0], 1)

            def read_q(g):
                b = 1 + g
                act.wait_ge(units_done, 8 * (b + 1))
                act.wait_ge(att_cleared, 1)
                if g:
                    act.wait_ge(scored, 4 * g)
                nc.scalar.activation(qsq, acc[:, b % 2], ACT.Square).then_inc(q_squared, 1)
                for half in range(2):
                    hp = slice(HEAD * half, HEAD * half + HEAD)
                    last = nc.scalar.copy(
                        qbd[hp, :, :, HEAD * half:HEAD * half + HEAD].rearrange("p t n q -> p (t n) q"),
                        acc[hp, b % 2].rearrange("p t (n q) -> p (t n) q", q=HEAD))
                last.then_inc(acc_read[b % 2], 1)

            def bias_of(j):
                if j >= 2:
                    act.wait_ge(biased, j - 1)
                nc.scalar.activation(abias[j % 2], dist, ACT.Copy, scale=slopes[:, j:j + 1]).then_inc(abias_made, 1)

            def exps(j):
                act.wait_ge(negmax_made, j + 1)
                if j >= 2:
                    act.wait_ge(p_turned, j - 1)
                for n in range(NWIN):
                    k0 = HEAD if n == 0 else 0
                    nc.scalar.activation(pr[j % 2][:, n, k0:], sc[j % 2][:, n, k0:], ACT.Exp,
                                         bias=negmax[j % 2][:, n:n + 1], accum_out=expsum[j % 2][:, n:n + 1])
                nc.scalar.activation(sinkexp[j % 2], negmax[j % 2], ACT.Exp, bias=sinkt[:, j:j + 1])\
                    .then_inc(exp_made, 1)

            def copy_turned(j):
                act.wait_ge(p_turned, j + 1)
                if j >= 2:
                    act.wait_ge(o_summed, j - 1)
                nc.scalar.copy(pt[j % 2], aux[:, 1, :].rearrange("p (n q) -> p n q", n=NWIN)).then_inc(p_copied, 1)

            def o_hi(j):
                act.wait_ge(o_summed, j + 1)
                nc.scalar.copy(a_hi[:, j, :], aux[:, 2, S * (j % 2):S * (j % 2) + S]).then_inc(a_hi_made, 1)

            def after_out(b, block, sub):
                act.wait_ge(acc_read[block % 2], block // 2 + 1)
                square_x(sub, b)

            def attn_after(u):
                b, s = divmod(u, 8)
                if b == 1 and s == 1:
                    act.wait_ge(k_summed, 1)
                    nc.scalar.activation(krstd, aux[:, 0, :], ACT.Sqrt, bias=epst[:], scale=1.0 / HEAD)\
                        .then_inc(k_root, 1)
                if b == 1 and s in (2, 3):
                    act.wait_ge(v_turned, s - 1)
                    nc.scalar.copy(vtok[:, 2 * (s - 2):2 * (s - 2) + 2, :],
                                   aux[:, 1, :].rearrange("p (n d) -> p n d", n=2)).then_inc(v_copied, 1)
                if u == 10:
                    act.wait_ge(k_normed, 1)
                    kd = kdup.rearrange("p (m two) s -> p two m s", two=2)
                    for half in range(2):
                        for to in range(2):
                            act.dma_start(kd[HEAD * to:HEAD * to + HEAD, half], kraw[HEAD * half:HEAD * half + HEAD])\
                                .then_inc(kdup_loaded, 16)
                if u in COPY_AT:
                    copy_turned(COPY_AT[u])
                if u in SCORES_AT:
                    bias_of(SCORES_AT[u])
                if u in EXP_AT:
                    exps(EXP_AT[u])
                if u in STAT_AT:
                    act.wait_ge(q_summed, STAT_AT[u] + 1)
                    nc.scalar.activation(qroot[:], QSTAT, ACT.Sqrt, bias=epst[0:2 * BT], scale=1.0 / HEAD)\
                        .then_inc(q_root, 1)
                if u in VALUES_AT and u % 8 < 7:
                    o_hi(VALUES_AT[u])

            def attn_sums_after(u):
                if u in VALUES_AT and u % 8 == 7:
                    o_hi(VALUES_AT[u])
                if u == 7:
                    read_kv()
                elif u % 8 == 7 and u // 8 < QKV_BLOCKS:
                    read_q(u // 8 - 1)
                if u in OUT_DONE:
                    after_out(OUT_DONE[u], QKV_BLOCKS + OUT_DONE[u], 1)

            split_stretch(ATTN, lambda: start_norm(0), attn_sums_after, norm=0, later=attn_after)

            def ffn(layer, start):
                sub = 2 * layer + 1
                after_last = start
                for ph, (up, down) in enumerate(FFN[layer]):
                    gp, upp = up.block0 % 2, (up.block0 + 1) % 2

                    def after_up(i):
                        act.wait_ge(acc_read[upp], (up.block0 + 1) // 2 + 1 + i)
                        nc.scalar.copy(a_hi[:, bass.ds(4 * i, 4), :], hid).then_inc(a_hi_made, 1)

                    def after_gate(i):
                        act.wait_ge(units_done, up.unit0 + up.units * i + 8)
                        act.wait_ge(acc_read[upp], (up.block0 + 1) // 2 + i)
                        nc.scalar.activation(gate, acc[:, gp], ACT.Silu).then_inc(acc_read[gp], 1)

                    def body(i, after_last, norm):
                        def after_unit(u):
                            if u == 7:
                                after_gate(i)
                        split_stretch(up, after_last, after_unit, i, sub if norm else None)

                    body(0, after_last, ph == 0)
                    with act.Fori(1, up.repeat) as i:
                        body(i, lambda: after_up(i - 1), False)

                    def after_down(u):
                        b, s = divmod(u, down.block_units)
                        if ph == 2 and s == down.block_units - 1 and layer == 0:
                            after_out(b, down.block0 + b, 2)
                        if ph == 2 and layer == 1 and u in OUT_TURNS:
                            store_block(OUT_TURNS.index(u))

                    split_stretch(down, lambda: after_up(up.repeat - 1), after_down)
                    after_last = lambda: None

            def store_block(b):
                act.wait_ge(out_turned, b + 1)
                if b >= 2:
                    act.wait_ge(out_stored[b % 2], 16)
                nc.scalar.copy(x_out[b % 2], aux[:, 0:2, :]).then_inc(out_copied, 1)

            def next_norm(sub, last_block):
                def f():
                    square_tiles(sub, last_block)
                    start_norm(sub)
                return f

            ffn(0, next_norm(1, ATTN.end[2] - 1))

            def sgu_after(u):
                b, s = divmod(u, 8)
                block = SGU.block0 + b
                par = block % 2
                if s == 7 and b < 4:
                    act.wait_ge(units_done, SGU.unit0 + u + 1)
                    nc.scalar.activation(vbuf[:, 4 * b:4 * b + 4, :], acc[:, par], ACT.Gelu).then_inc(acc_read[par], 1)
                    act.wait_ge(acc_read[par], block // 2 + 1)
                    square_block(V_BLOCKS + b, vbuf[:, 4 * b:4 * b + 4, :])
                elif s == 7 and b < 8:
                    act.wait_ge(units_done, SGU.unit0 + u + 1)
                    if b > 4:
                        act.wait_ge(y_made, b - 4)
                    nc.scalar.activation(ugate, acc[:, par], ACT.Gelu).then_inc(acc_read[par], 1)
                    act.wait_ge(y_made, b - 3)
                    nc.scalar.copy(a_hi[:, 4 * (b - 4):4 * (b - 4) + 4, :], yf).then_inc(a_hi_made, 1)
                elif s == 7:
                    after_out(b - 8, block, 3)
                if u == 32:
                    act.wait_ge(vstat_summed, 1)
                    nc.scalar.activation(vroot, VSTAT, ACT.Sqrt, bias=epst[:], scale=1.0 / D).then_inc(vroot_made, 1)
                if u in V_TURN_AT:
                    k = V_TURN_AT[u]
                    act.wait_ge(vrstd_made, 1)
                    act.wait_ge(vt_turned, k + 1)
                    for n in range(2):
                        last = nc.scalar.activation(v_tokens(k)[:, n, :], aux[:, n, :], ACT.Copy,
                                                    scale=vrstd[:, n:n + 1])
                    last.then_inc(vt_copied, 1)

            split_stretch(SGU, next_norm(2, FFN0[2][1].end[2] - 1), sgu_after, norm=2)
            ffn(1, next_norm(3, SGU.end[2] - 1))
            for b in range(OUT_BLOCKS):
                if OUT_TURNS[b] >= FFN1[2][1].units - AHEAD:
                    store_block(b)

        @block.vector
        def _(dve):
            def reduce_block(n, b, read_by, times):
                dve.wait_ge(squared, n + 1)
                if times:
                    dve.wait_ge(read_by, times)
                nc.vector.tensor_reduce(out=parts[:, b, :], in_=sq.rearrange("p t s -> p s t"), axis=AX.X,
                                        op=ALU.add).then_inc(parts_made, 1)

            def reduce_x(sub, b):
                reduce_block(NORM_BLOCKS[sub] + b, b, *((vstat_summed, 1) if sub == 3 else (stat_summed, sub)))

            def ada_step(q, s, slot, round_, looped, after_loop, i=0):
                parts_n = ada_parts(q)
                into = ada[:, 0 if looped else q % 2, s % parts_n, :]
                if s % KC == 0:
                    dve.wait_ge(loaded[slot], 16 * round_)
                weight, scale = ring[slot][:, s % KC, :], c_act[:, s:s + 1]
                if s < parts_n:
                    if looped or after_loop or q >= 2:
                        dve.wait_ge(ada_summed, q + i - (0 if looped or after_loop else 1))
                    nc.vector.tensor_scalar(into, weight, scale, None, ALU.mult).then_inc(ada_steps, 1)
                else:
                    dve.wait_ge(ada_steps, DT * (q + i) + s - parts_n + 1)
                    nc.vector.scalar_tensor_tensor(out=into, in0=weight, scalar=scale, in1=into,
                                                   op0=ALU.mult, op1=ALU.add).then_inc(ada_steps, 1)

            def make_mod(q, i=0):
                cols = bass.ds(BT * q + BT * i, BT)
                dve.wait_ge(ada_summed, q + i + 1)
                nc.vector.tensor_tensor(mod[:, cols], ADA_COLS[:, cols], bias_t[:, cols], ALU.add)\
                    .then_inc(mod_made, 1)

            def update_x(layer, m, b, block, end_unit, by_tile=False):
                g = mod_col(layer, m, 4 * b)
                dve.wait_ge(units_done, end_unit)
                dve.wait_ge(mod_made, vector_made(layer, m))
                for t in range(BT):
                    xt = x[:, 4 * b + t, :]
                    last = nc.vector.scalar_tensor_tensor(out=xt, in0=acc[:, block % 2, t, :],
                                                          scalar=mod[:, g + t:g + t + 1], in1=xt,
                                                          op0=ALU.mult, op1=ALU.add)
                    if by_tile and t < BT - 1:
                        last.then_inc(x_updated, 1)
                last.then_inc(acc_read[block % 2], 1)

            def norm_x(sub, k):
                n = HP * sub + k
                if k == 0:
                    dve.wait_ge(root_made, sub + 1)
                    nc.vector.reciprocal(rstd[:], root[:]).then_inc(rstd_made, 1)
                    dve.wait_ge(rstd_made, sub + 1)
                if k >= 4:
                    dve.wait_ge(hf_made, n - 3)
                nc.vector.tensor_tensor(xr_piece[k % 4], x[:, HT * k:HT * k + HT, :], rows_over(rstd[:], HT), ALU.mult)\
                    .then_inc(xr_made, 1)

            def h_lo_of(sub, k):
                dve.wait_ge(h_hi_made, HP * sub + k + 1)
                nc.vector.tensor_tensor(h_lo[:, HT * k:HT * k + HT, :], hf_piece[k % 4],
                                        h_hi[:, HT * k:HT * k + HT, :].bitcast(F32), ALU.subtract).then_inc(h_made, 1)

            def start_norm(sub):
                if sub:
                    norm_x(sub, 0)
                    norm_x(sub, 1)
                h_lo_of(sub, 0)
                if sub:
                    norm_x(sub, 2)
                h_lo_of(sub, 1)

            def start_first():
                make_mod(PRO_ITEMS // KI - 1)
                start_norm(0)

            def split_lo(st, u, i=0):
                slot = st.places("w")[u][0]
                dve.wait_ge(hi_made, st.unit0 + st.units * i + u + 1)
                nc.vector.tensor_tensor(w_lo[u % SPLIT][:], ring[slot][:], w_hi[u % SPLIT][:].bitcast(F32),
                                        ALU.subtract).then_inc(lo_made, 1)

            def split_stretch(st, after_last, after_unit, i=0, looped=False, after_loop=False,
                              norm=None, later=lambda u: None):
                step, sums = 0, st.sums_after()
                if looped:
                    sums = {BODY_SUM_AFTER: 0} if st.ada_items else {}
                for u in range(st.units):
                    if u == (AHEAD - 1 if st.unit0 else 1):
                        after_last()
                    if u >= AHEAD:
                        after_unit(u - AHEAD)
                    split_lo(st, u, i)
                    if norm is not None and 2 <= u - 1 < HP:
                        if u < HP:
                            norm_x(norm, u)
                        h_lo_of(norm, u - 1)
                    if u >= AHEAD:
                        later(u - AHEAD)
                    if u - AHEAD in sums:
                        make_mod(st.ada0 // KI + sums[u - AHEAD], i)
                    for _ in range(st.steps[u]):
                        q, s = divmod(step, DT)
                        ada_step(st.ada0 // KI + q, s, *st.places("a", i)[step // KC], looped,
                                 after_loop and q == 0, i)
                        step += 1

            for q in range(PRO_ITEMS // KI):
                for s in range(DT):
                    if q == 0 and s == 0:
                        dve.wait_ge(c_made, 1)
                    n = KI * q + s // KC
                    ada_step(q, s, n % RING, n // RING + 1, False, False)
                    if q == 7 and s == DT // 2:
                        for k in range(3):
                            norm_x(0, k)
                if q == 1:
                    dve.wait_ge(vecs_copied, 1)
                    scale_bias = bias_t[:].rearrange("p (l h m t) -> p (l h) m t", l=2, h=2, t=DT)[:, :, SC1, :]
                    nc.vector.tensor_scalar(scale_bias, scale_bias, 1.0, None, ALU.add).then_inc(bias_made, 1)
                    dve.wait_ge(bias_made, 1)
                if q:
                    make_mod(q - 1)
                if 3 <= q < 7:
                    reduce_x(0, q - 3)
            def norm_k():
                dve.wait_ge(vecs_loaded, 16 * 9)
                nc.vector.scalar_tensor_tensor(out=kgain[:], in0=gains[:, 0:1], scalar=HEAD ** -0.5,
                                               in1=gains[:, 1:2], op0=ALU.mult, op1=ALU.mult).then_inc(kgain_made, 1)
                dve.wait_ge(k_root, 1)
                nc.vector.reciprocal(krstd, krstd).then_inc(k_recip, 1)
                dve.wait_ge(k_recip, 1)
                dve.wait_ge(kgain_made, 1)
                kf = kraw.rearrange("p m s -> p (m s)")
                nc.vector.scalar_tensor_tensor(out=kf, in0=kf, scalar=kgain[:], in1=krstd,
                                               op0=ALU.mult, op1=ALU.mult).then_inc(k_normed, 1)

            def softmax_in(j):
                t, n_pairs = j % 4, PAIRS // KV_HEADS
                dve.wait_ge(scored, j + 1)
                dve.wait_ge(abias_made, j + 1)
                if j >= 2:
                    dve.wait_ge(exp_made, j - 1)
                for n in range(NWIN):
                    k0 = HEAD if n == 0 else 0
                    last = nc.vector.scalar_tensor_tensor(
                        out=sc[j % 2][:, n, k0:], in0=aux[:, 0, P * n + k0:P * n + P],
                        scalar=qrstd[:, n_pairs * t + n:n_pairs * t + n + 1], in1=abias[j % 2][:, k0:],
                        op0=ALU.mult, op1=ALU.add)
                last.then_inc(biased, 1)
                dve.wait_ge(biased, j + 1)
                nc.vector.tensor_reduce(out=smax, in_=sc[j % 2], axis=AX.X, op=ALU.max).then_inc(max_made, 1)
                dve.wait_ge(max_made, j + 1)
                nc.vector.tensor_scalar(negmax[j % 2], smax, sinkt[:, j:j + 1], -1.0, ALU.max, ALU.mult)\
                    .then_inc(negmax_made, 1)

            def softmax_out(j):
                dve.wait_ge(exp_made, j + 1)
                nc.vector.tensor_tensor(den, expsum[j % 2], sinkexp[j % 2], ALU.add).then_inc(den_made, 1)
                dve.wait_ge(den_made, j + 1)
                nc.vector.reciprocal(inv, den).then_inc(inv_made, 1)
                dve.wait_ge(inv_made, j + 1)
                nc.vector.tensor_tensor(pr[j % 2], pr[j % 2], inv.unsqueeze(2).to_broadcast([P, NWIN, P]), ALU.mult)\
                    .then_inc(probs_made, 1)

            def o_lo(j):
                dve.wait_ge(a_hi_made, j + 1)
                nc.vector.tensor_tensor(a_lo[:, j, :], aux[:, 2, S * (j % 2):S * (j % 2) + S],
                                        a_hi[:, j, :].bitcast(F32), ALU.subtract).then_inc(a_made, 1)

            def after_out(layer, m, b, block, end_unit, sub):
                last_block = b == OUT_BLOCKS - 1
                update_x(layer, m, b, block, end_unit, last_block)
                if not last_block:
                    reduce_x(sub, b)

            def attn_after(u):
                b, s = divmod(u, 8)
                if b == 1 and s == 1:
                    norm_k()
                if u in STAT_TURN_AT:
                    dve.wait_ge(q_turned, STAT_TURN_AT[u] + 1)
                    for half in range(2):
                        hp = slice(HEAD * half, HEAD * half + HEAD)
                        last = nc.vector.reciprocal(qrstd[hp].rearrange("p (t n) -> p t n", t=BT),
                                                    QTURNED[hp].rearrange("p (n t h) -> p h t n", n=NWIN, t=BT)[:, half])
                    last.then_inc(q_recip, 1)
                if u in SOFTMAX_OUT_AT:
                    softmax_out(SOFTMAX_OUT_AT[u])
                if u in VALUES_AT:
                    o_lo(VALUES_AT[u])

            def out_after(u):
                if u in SOFTMAX_IN_AT:
                    j = SOFTMAX_IN_AT[u]
                    dve.wait_ge(q_recip, j // 4 + 1)
                    softmax_in(j)
                if u in OUT_DONE:
                    after_out(0, G1, OUT_DONE[u], QKV_BLOCKS + OUT_DONE[u], u + 1, 1)

            split_stretch(ATTN, start_first, out_after, norm=0, later=attn_after)

            def ffn(layer, start):
                sub, a0 = 2 * layer + 1, A_COUNT[layer]
                after_last = start
                done = 0
                for ph, (up, down) in enumerate(FFN[layer]):
                    gp, upp = up.block0 % 2, (up.block0 + 1) % 2

                    def multiply_up(i):
                        dve.wait_ge(units_done, up.unit0 + up.units * (i + 1))
                        dve.wait_ge(acc_read[gp], up.block0 // 2 + 1 + i)
                        nc.vector.tensor_tensor(hid, acc[:, upp], gate, ALU.mult).then_inc(acc_read[upp], 1)

                    def hidden_lo(i):
                        dve.wait_ge(a_hi_made, a0 + done + i + 1)
                        nc.vector.tensor_tensor(a_lo[:, bass.ds(4 * i, 4), :], hid,
                                                a_hi[:, bass.ds(4 * i, 4), :].bitcast(F32), ALU.subtract)\
                            .then_inc(a_made, 1)

                    def body(i, after_last, norm, previous=None):
                        def after_unit(u):
                            if u == 0 and previous is not None:
                                hidden_lo(previous)
                        split_stretch(up, after_last, after_unit, i, looped=True, norm=sub if norm else None)

                    body(0, after_last, ph == 0)
                    with dve.Fori(1, up.repeat) as i:
                        body(i, lambda: multiply_up(i - 1), False, i - 1)

                    def after_block(b, down=down, ph=ph):
                        end = down.unit0 + down.block_units * (b + 1)
                        if ph == 2 and layer == 0:
                            after_out(layer, G2, b, down.block0 + b, end, 2)
                        else:
                            update_x(layer, G2, b, down.block0 + b, end)

                    def after_down(u):
                        if u == 0:
                            hidden_lo(up.repeat - 1)
                        if (u + 1) % down.block_units == 0:
                            after_block(u // down.block_units)

                    split_stretch(down, lambda: multiply_up(up.repeat - 1), after_down, after_loop=True)
                    done += up.repeat
                    after_last = lambda after_block=after_block: after_block(3)
                return after_last

            def next_norm(sub, last):
                def f():
                    last()
                    start_norm(sub)
                return f

            last = ffn(0, next_norm(1, lambda: after_out(
                0, G1, 3, ATTN.end[2] - 1, ATTN.units, 1)))

            def sgu_after(u):
                b, s = divmod(u, 8)
                block = SGU.block0 + b
                if s == 7 and b < 4:
                    reduce_block(V_BLOCKS + b, b, stat_summed, 3)
                elif s == 7 and b < 8:
                    dve.wait_ge(acc_read[block % 2], block // 2 + 1)
                    dve.wait_ge(sv_made, b - 3)
                    nc.vector.tensor_tensor(yf, ugate, vbuf[:, 4 * (b - 4):4 * (b - 4) + 4, :], ALU.mult)\
                        .then_inc(y_made, 1)
                    dve.wait_ge(a_hi_made, A_SGU + b - 3)
                    nc.vector.tensor_tensor(a_lo[:, 4 * (b - 4):4 * (b - 4) + 4, :], yf,
                                            a_hi[:, 4 * (b - 4):4 * (b - 4) + 4, :].bitcast(F32), ALU.subtract)\
                        .then_inc(a_made, 1)
                elif s == 7:
                    after_out(1, G1, b - 8, block, SGU.unit0 + u + 1, 3)
                if u == 32:
                    dve.wait_ge(vroot_made, 1)
                    nc.vector.reciprocal(vrstd, vroot).then_inc(vrstd_made, 1)
                if u in V_TURN_AT:
                    k = V_TURN_AT[u]
                    dve.wait_ge(ws_turned, k + 1)
                    if k:
                        dve.wait_ge(mixed, k)
                    nc.vector.tensor_tensor(ws_t, aux[:, 2, :].rearrange("p (g t) -> p g t", g=4),
                                            rows_over(mask, 4), ALU.mult).then_inc(ws_masked, 1)
                if u in MIX_AT:
                    k = MIX_AT[u]
                    dve.wait_ge(mixed, k + 1)
                    dve.wait_ge(ws_loaded[k % 2], 32 * (k // 2 + 1))
                    for t in range(4):
                        last = nc.vector.scalar_tensor_tensor(
                            out=vbuf[:, 4 * k + t, :].rearrange("p (n t) -> p n t", n=2),
                            in0=MIXED[:, t, :].rearrange("p (n t) -> p n t", n=2),
                            scalar=vgain[:, 4 * k + t:4 * k + t + 1], in1=rows_over(bs_b[k % 2][:, t, :], 2),
                            op0=ALU.mult, op1=ALU.add)
                    last.then_inc(sv_made, 1)

            split_stretch(SGU, next_norm(2, last),
                          sgu_after, after_loop=True, norm=2)
            last = ffn(1, next_norm(3, lambda: after_out(
                1, G1, 3, SGU.end[2] - 1, SGU.end[1], 3)))
            last()

        @block.tensor
        def _(pe):
            def unit(st, u, act_hi, act_lo, kt, first, last_, par, i=0):
                pe.wait_ge(lo_made, st.unit0 + st.units * i + u + 1)
                hi, lo = w_hi[u % SPLIT], w_lo[u % SPLIT]
                for k in range(KC):
                    for t in range(BT):
                        cols, sums = slice(P * t, P * t + P), acc[:, par, t, :]
                        start = first and k == 0 and t % 2 == 0
                        stop = last_ and k == KC - 1
                        nc.tensor.matmul(sums, hi[:, k, cols], act_hi[:, kt + k, :], start=start, stop=False,
                                         skip_group_check=True)
                        nc.tensor.matmul(sums, hi[:, k, cols], act_lo[:, kt + k, :], start=False, stop=False,
                                         skip_group_check=True)
                        done = nc.tensor.matmul(sums, lo[:, k, cols], act_hi[:, kt + k, :], start=False, stop=stop,
                                                skip_group_check=True)
                done.then_inc(units_done, 1)

            def wait_sums_free(block, i=0):
                if block < 2:
                    pe.wait_ge(x_copied, 4)
                else:
                    pe.wait_ge(acc_read[block % 2], block // 2 + i)

            def ada_sum(q, looped, i=0):
                sums, parts_n = ada[:, 0 if looped else q % 2], ada_parts(q)
                pe.wait_ge(ada_steps, DT * (q + i + 1))
                if looped or q:
                    pe.wait_ge(mod_made, q + i)
                for t in range(BT):
                    for part in range(parts_n):
                        done = nc.tensor.matmul(ADA_COLS[:, bass.ds(BT * q + BT * i + t, 1)],
                                                sums[:, part, P * t:P * t + P], ones[:, 0:1],
                                                start=part == 0, stop=part == parts_n - 1, skip_group_check=True)
                done.then_inc(ada_summed, 1)

            def norm_stat(sub):
                by_tile = sub > 0
                blocks = 3 if by_tile else 4
                pe.wait_ge(parts_made, NORM_BLOCKS[sub] + blocks)
                for b in range(blocks):
                    done = nc.tensor.matmul(aux[:, 2, 0:S], ones, parts[:, b, :], start=b == 0, stop=b == 3)
                if by_tile:
                    for t in range(BT):
                        pe.wait_ge(tile_squared, BT * (sub - 1) + t + 1)
                        done = nc.tensor.matmul(aux[:, 2, 0:S], ones, sq[:, t, :], start=False, stop=t == BT - 1)
                done.then_inc(stat_summed, 1)

            def stay_warm(block, count):
                wait_sums_free(block)
                for n in range(count):
                    nc.tensor.matmul(acc[:, block % 2, 0, 0:P], ones, ones, start=True, stop=True,
                                     skip_group_check=True)

            pe.wait_ge(consts_loaded, 16)
            pe.wait_ge(rows_loaded, 16)
            nc.tensor.transpose(TURNED[:, 0:DT], rows[0:DT, 0, :], ident[0:DT, 0:DT]).then_inc(rows_turned, 1)
            pe.wait_ge(x_loaded, 16)
            for b in range(4):
                if b >= 2:
                    pe.wait_ge(x_copied, b - 1)
                for n in range(2):
                    for t in range(4):
                        done = nc.tensor.transpose(acc[:, b % 2, t, P * n:P * n + P],
                                                   x_tok[:, n, P * (4 * b + t):P * (4 * b + t) + P], ident)
                done.then_inc(x_turned, 1)
            pe.wait_ge(vecs_loaded, 16 * 9)
            pe.wait_ge(c_made, 1)
            nc.tensor.transpose(TURNED[:, DT:2 * DT], rows[0:DT, 1, :], ident[0:DT, 0:DT])
            for l in range(2):
                nc.tensor.transpose(TURNED[:, 2 * DT + MOD_COLS * l:2 * DT + MOD_COLS * (l + 1)],
                                    rows[0:MOD_COLS, 2 + l, :], ident[0:MOD_COLS, 0:MOD_COLS])
            for half in range(2):
                done = nc.tensor.matmul(TURNED[HEAD * half:HEAD * half + HEAD, 240:240 + PAIRS], ones[0:1, 0:HEAD],
                                        sink_row[0:1, half:HEADS:2], start=True, stop=True)
            done.then_inc(rows_turned, 1)
            for q in range(PRO_ITEMS // KI):
                if q == PRO_ITEMS // KI - 1:
                    norm_stat(0)
                ada_sum(q, False)

            def turn_v(r):
                if r:
                    pe.wait_ge(v_copied, r)
                for n in range(2):
                    for m in range(2):
                        key0 = HEAD * (2 * r + n)
                        done = nc.tensor.transpose(aux[:, 1, S * n + P * m:S * n + P * m + P],
                                                   vpad[:, m, key0:key0 + P], ident)
                done.then_inc(v_turned, 1)

            def q_stat(g):
                pe.wait_ge(q_squared, g + 1)
                if g:
                    pe.wait_ge(a_made, 4 * g - 3)
                else:
                    pe.wait_ge(root_made, 1)
                for t in range(BT):
                    done = nc.tensor.matmul(QSTAT, picks[:, 2 * BT * t:2 * BT * t + 2 * BT], qsq[:, t, :],
                                            start=t == 0, stop=t == BT - 1)
                done.then_inc(q_summed, 1)

            def q_stat_turned(g):
                pe.wait_ge(q_root, g + 1)
                for n in range(NWIN):
                    for half in range(2):
                        done = nc.tensor.matmul(
                            QTURNED[HEAD * half:HEAD * half + HEAD, 2 * BT * n:2 * BT * n + 2 * BT],
                            qroot[:, HEAD * n:HEAD * n + HEAD], ident[0:2 * BT, 0:2 * BT], start=True, stop=True,
                            skip_group_check=True)
                done.then_inc(q_turned, 1)

            def scores(j):
                g, t = divmod(j, 4)
                pe.wait_ge(kdup_loaded, 64)
                if t == 0:
                    pe.wait_ge(acc_read[(1 + g) % 2], (1 + g) // 2 + 1)
                if j:
                    pe.wait_ge(biased, j)
                for n in range(NWIN):
                    k0 = HEAD if n == 0 else 0
                    done = nc.tensor.matmul(aux[:, 0, P * n + k0:P * n + P], qbd[:, t, n, :],
                                            kdup[:, g, HEAD * (n - 1) + k0:HEAD * (n + 1)], start=True, stop=True,
                                            skip_group_check=True)
                done.then_inc(scored, 1)

            def turn_p(j):
                pe.wait_ge(probs_made, j + 1)
                if j:
                    pe.wait_ge(p_copied, j)
                else:
                    pe.wait_ge(v_copied, 2)
                for n in range(NWIN):
                    done = nc.tensor.transpose(aux[:, 1, P * n:P * n + P], pr[j % 2][:, n, :], ident)
                done.then_inc(p_turned, 1)

            def values(j):
                g = j // 4
                pe.wait_ge(p_copied, j + 1)
                if j:
                    pe.wait_ge(a_made, j)
                pe.wait_ge(q_recip, min((j + 3) // 4 + 1, KV_HEADS))
                for n in range(NWIN):
                    for half in range(2):
                        col = S * (j % 2) + HEAD * n
                        done = nc.tensor.matmul(aux[HEAD * half:HEAD * half + HEAD, 2, col:col + HEAD],
                                                vtok[:, n, HEAD * g:HEAD * g + HEAD],
                                                pt[j % 2][:, n, HEAD * half:HEAD * half + HEAD], start=True, stop=True,
                                                skip_group_check=True)
                done.then_inc(o_summed, 1)

            def attn_after(u):
                b, s = divmod(u, 8)
                if b == 1 and s == 1:
                    pe.wait_ge(acc_read[0], 1)
                    nc.tensor.matmul(aux[:, 0, :], head_ones, ksq.rearrange("p m s -> p (m s)"), start=True,
                                     stop=True).then_inc(k_summed, 1)
                if b == 1 and s in (2, 3):
                    turn_v(s - 2)
                if u in VALUES_AT:
                    values(VALUES_AT[u])
                if u in STAT_TURN_AT:
                    q_stat_turned(STAT_TURN_AT[u])
                if u in STAT_AT:
                    q_stat(STAT_AT[u])
                if u in SCORES_AT:
                    scores(SCORES_AT[u])
                if u in TURN_AT:
                    turn_p(TURN_AT[u])

            def run(st, activations, after_unit, i=0, looped=False, order=None):
                sums = st.sums_after() if not looped else {}
                for u in range(st.units):
                    b, v = divmod(u, st.block_units)
                    if order:
                        b, v = order[u]
                    block = st.block0 + b
                    if v == 0:
                        wait_sums_free(block, i)
                    hi, lo, wait_group = activations(b)
                    if wait_group is not None:
                        wait_group(v)
                    unit(st, u, hi, lo, KC * v, v == 0, v == st.block_units - 1, block % 2, i)
                    if u in sums:
                        ada_sum(st.ada0 // KI + sums[u], False)
                    if looped and st.ada_items and u == BODY_SUM_AFTER:
                        ada_sum(st.ada0 // KI, True, i)
                    after_unit(u)

            def use_h(sub, first):
                wait = (lambda v: pe.wait_ge(h_made, HP * sub + v + 1)) if first else None
                return h_hi, h_lo, wait

            def use_a(count, per_group, first):
                wait = (lambda v: pe.wait_ge(a_made, count + per_group * (v // 2 + 1))) if first else None
                return a_hi, a_lo, wait

            stay_warm(0, 12)
            run(ATTN, lambda b: use_h(0, b == 0) if b < QKV_BLOCKS else use_a(0, 4, b == QKV_BLOCKS), attn_after,
                order=ATTN_UNITS)

            def ffn(layer):
                sub, a0 = 2 * layer + 1, A_COUNT[layer]
                norm_stat(sub)
                stay_warm(FFN[layer][0][0].block0, 24)
                for ph, (up, down) in enumerate(FFN[layer]):
                    run(up, lambda b: use_h(sub, ph == 0 and b == 0), lambda u: None, looped=True)
                    with pe.Fori(1, up.repeat) as i:
                        run(up, lambda b: use_h(sub, False), lambda u: None, i, looped=True)

                    def after_down(u):
                        if layer == 1 and ph == 2 and u in OUT_TURNS:
                            turn_out(OUT_TURNS.index(u))
                    run(down, lambda b: use_a(a0, 1, b == 0), after_down)
                    a0 += up.repeat

            def turn_out(b):
                block = FFN1[2][1].block0 + b
                pe.wait_ge(acc_read[block % 2], block // 2 + 1)
                if b:
                    pe.wait_ge(out_copied, b)
                for n in range(2):
                    for t in range(4):
                        done = nc.tensor.transpose(aux[:, n, P * t:P * t + P], x[:, 4 * b + t, P * n:P * n + P], ident)
                done.then_inc(out_turned, 1)

            ffn(0)

            def sgu_after(u):
                if u == 32:
                    pe.wait_ge(parts_made, V_BLOCKS + 4)
                    for n in range(2):
                        for b in range(4):
                            done = nc.tensor.matmul(VSTAT[:, n:n + 1], parts[:, b, P * n:P * n + P], ones[:, 0:1],
                                                    start=b == 0, stop=b == 3, skip_group_check=True)
                    done.then_inc(vstat_summed, 1)
                if u in V_TURN_AT:
                    k = V_TURN_AT[u]
                    pe.wait_ge(ws_loaded[k % 2], 32 * (k // 2 + 1))
                    if k:
                        pe.wait_ge(ws_masked, k)
                    else:
                        pe.wait_ge(vroot_made, 1)
                    for t in range(4):
                        done = nc.tensor.transpose(aux[:, 2, P * t:P * t + P], ws_raw[k % 2][:, t, :], ident)
                    done.then_inc(ws_turned, 1)
                    if k:
                        pe.wait_ge(sv_made, k)
                    for n in range(2):
                        for t in range(4):
                            done = nc.tensor.transpose(aux[:, n, P * t:P * t + P],
                                                       vbuf[:, 4 * k + t, P * n:P * n + P], ident)
                    done.then_inc(vt_turned, 1)
                if u in MIX_AT:
                    k = MIX_AT[u]
                    pe.wait_ge(vt_copied, k + 1)
                    pe.wait_ge(ws_masked, k + 1)
                    for t in range(4):
                        for n in range(2):
                            done = nc.tensor.matmul(MIXED[:, t, P * n:P * n + P], v_tokens(k)[:, n, P * t:P * t + P],
                                                    ws_t[:, t, :], start=True, stop=True, skip_group_check=True)
                    done.then_inc(mixed, 1)

            norm_stat(2)
            stay_warm(SGU.block0, 24)
            run(SGU, lambda b: use_h(2, b == 0) if b < 2 * OUT_BLOCKS else use_a(A_SGU, 1, b == 2 * OUT_BLOCKS),
                sgu_after)
            ffn(1)
            for b in range(OUT_BLOCKS):
                if OUT_TURNS[b] >= FFN1[2][1].units:
                    turn_out(b)


def constant_tiles():
    i = np.arange(P)
    half = i // HEAD
    tiles = np.zeros((P, 6, P), np.float32)
    tiles[:, 0] = np.eye(P)
    tiles[:, 1] = 1
    tiles[:, 2] = half[:, None] == half[None, :]
    tiles[:, 3] = np.abs(i[:, None] % HEAD + HEAD - i[None, :])
    tiles[:, 4] = half[None, :] >= half[:, None]
    for t in range(BT):
        for h in range(2):
            tiles[half == h, 5, 2 * BT * t + 2 * t + h] = 1
    return tiles


def constant_slopes():
    slope = -(2.0 ** (-8.0 * np.arange(1, HEADS + 1) / HEADS)).astype(np.float32)
    return np.ascontiguousarray(np.repeat(slope.reshape(PAIRS, 2).T, HEAD, axis=0))


INPUTS = ["x", "c", "w_ada", "b_ada", "attn_w_qkv", "attn_q_gain", "attn_k_gain", "attn_sinks", "attn_w_o",
          "sgu_w_in", "sgu_v_gain", "sgu_w_s", "sgu_b_s", "sgu_w_out", "ffn_w_gate", "ffn_w_up", "ffn_w_down"]


def kernel(**inputs):
    import concourse.bacc as bacc
    from concourse.bass_utils import run_bass_kernel_spmd

    nc = bacc.Bacc("TRN2", target_bir_lowering=False, num_devices=1)
    arrays = {f"in_{name}": np.ascontiguousarray(inputs[name]) for name in INPUTS}
    arrays["const_tiles"] = constant_tiles()
    arrays["const_slopes"] = constant_slopes()
    args = [nc.dram_tensor(name, a.shape, F32, kind="ExternalInput").ap() for name, a in arrays.items()]
    result = nc.dram_tensor("out", (1, S, D), F32, kind="ExternalOutput").ap()
    trunk(nc, *args, result)
    r = run_bass_kernel_spmd(nc, [arrays], core_ids=[0])
    return r.results[0]["out"]
```
